# Optimizing a Trainium2 kernel written in Bass

```python
import jax, jax.numpy as jnp
from jax import lax
import numpy as np

D_MODEL = 1024
BATCH = 1
SEQ = 512
DEPTH = 1

D_MIX = D_MODEL
CONV_CH = D_MIX // 2
CONV_K = 31
SB_HEADS = 8
SB_HEAD_DIM = (D_MIX - CONV_CH) // SB_HEADS
SB_WIDTH = SB_HEADS * SB_HEAD_DIM
BLOCK_Q = 128
MEM_LEN = 256
MEM_HEADS = 4
MEM_HEAD_DIM = D_MODEL // MEM_HEADS
D_FF = ((8 * D_MODEL // 3 + 127) // 128) * 128
FFN_K = 3
IN_WIDTH = 2 * CONV_CH + 3 * SB_WIDTH
DEEPNORM_ALPHA = (2.0 * DEPTH) ** 0.25
DEEPNORM_BETA = (8.0 * DEPTH) ** -0.25
LN_EPS = 1e-5

kernel_name = "hybrid_conformer_stickbreak_deepnorm_trunk"

def layer_norm(x, g, b):
    xf = x.astype(jnp.float32)
    mu = jnp.mean(xf, axis=-1, keepdims=True)
    var = jnp.mean(jnp.square(xf - mu), axis=-1, keepdims=True)
    y = (xf - mu) * lax.rsqrt(var + LN_EPS)
    return (y * g.astype(jnp.float32) + b.astype(jnp.float32)).astype(x.dtype)

def causal_dwconv(x, w, b):
    k = w.shape[0]
    y = lax.conv_general_dilated(
        x, w[:, None, :].astype(x.dtype), window_strides=(1,), padding=[(k - 1, 0)],
        dimension_numbers=('NWC', 'WIO', 'NWC'), feature_group_count=x.shape[-1])
    return y + b

def stick_breaking_attention(q, k, v):
    bsz, seq, nh, dh = q.shape
    nb = seq // BLOCK_Q
    scale = dh ** -0.5
    qf = q.astype(jnp.float32).transpose(0, 2, 1, 3)
    kf = k.astype(jnp.float32).transpose(0, 2, 1, 3)
    vf = v.astype(jnp.float32).transpose(0, 2, 1, 3)
    q_blocks = qf.reshape(bsz, nh, nb, BLOCK_Q, dh).transpose(2, 0, 1, 3, 4)
    key_pos = jnp.arange(seq)

    def one_block(args):
        q_blk, blk = args
        q_pos = blk * BLOCK_Q + jnp.arange(BLOCK_Q)
        visible = key_pos[None, :] < q_pos[:, None]
        z = jnp.einsum('bhqd,bhkd->bhqk', q_blk, kf) * scale
        log_keep = jnp.where(visible, jax.nn.log_sigmoid(-z), 0.0)
        later = lax.cumsum(log_keep, axis=3, reverse=True) - log_keep
        a = jnp.where(visible, jnp.exp(jax.nn.log_sigmoid(z) + later), 0.0)
        return jnp.einsum('bhqk,bhkd->bhqd', a, vf)

    out = lax.map(one_block, (q_blocks, jnp.arange(nb)))
    out = out.transpose(1, 0, 3, 2, 4).reshape(bsz, seq, nh * dh)
    return out.astype(q.dtype)

def hybrid_mixer(h, w_in, conv_w, conv_b, conv_ln_g, conv_ln_b, w_out):
    bsz, seq, _ = h.shape
    proj = h @ w_in
    glu_a, glu_g, q, k, v = jnp.split(
        proj, [CONV_CH, 2 * CONV_CH, 2 * CONV_CH + SB_WIDTH, 2 * CONV_CH + 2 * SB_WIDTH], axis=-1)
    u = glu_a * jax.nn.sigmoid(glu_g)
    u = causal_dwconv(u, conv_w, conv_b)
    u = jax.nn.silu(layer_norm(u, conv_ln_g, conv_ln_b))
    heads = lambda t: t.reshape(bsz, seq, SB_HEADS, SB_HEAD_DIM)
    a = stick_breaking_attention(heads(q), heads(k), heads(v))
    return jnp.concatenate([u, a], axis=-1) @ w_out

def memory_cross_attention(h, mem, wq, wk, wv, wo):
    bsz, seq, _ = h.shape
    q = (h @ wq).reshape(bsz, seq, MEM_HEADS, MEM_HEAD_DIM).astype(jnp.float32)
    k = (mem @ wk).reshape(bsz, -1, MEM_HEADS, MEM_HEAD_DIM).astype(jnp.float32)
    v = (mem @ wv).reshape(bsz, -1, MEM_HEADS, MEM_HEAD_DIM).astype(jnp.float32)
    s = jnp.einsum('bqhd,bmhd->bhqm', q, k) * (MEM_HEAD_DIM ** -0.5)
    p = jax.nn.softmax(s, axis=-1)
    o = jnp.einsum('bhqm,bmhd->bqhd', p, v).reshape(bsz, seq, D_MODEL).astype(h.dtype)
    return o @ wo

def conv_gated_ffn(h, w_up, conv_w, conv_b, w_down):
    up = causal_dwconv(h @ w_up, conv_w, conv_b)
    val, gate = jnp.split(up, 2, axis=-1)
    return (jax.nn.silu(gate) * val) @ w_down

def setup_inputs(seed: int = 0) -> dict:
    key = jax.random.key(seed)
    ks = jax.random.split(key, 32)
    nrm = lambda k, shape, s: jax.random.normal(k, shape, jnp.float32) * s
    gain = lambda k, n: 1.0 + 0.05 * jax.random.normal(k, (DEPTH, n), jnp.float32)
    bias = lambda k, n: 0.01 * jax.random.normal(k, (DEPTH, n), jnp.float32)
    col = jnp.arange(IN_WIDTH)
    v_scale = jnp.where(col >= 2 * CONV_CH + 2 * SB_WIDTH, DEEPNORM_BETA, 1.0).astype(jnp.float32)
    w_in = nrm(ks[2], (DEPTH, D_MODEL, IN_WIDTH), D_MODEL ** -0.5) * v_scale
    return {
        "x": nrm(ks[0], (BATCH, SEQ, D_MODEL), 1.0),
        "mem": nrm(ks[1], (BATCH, MEM_LEN, D_MODEL), 1.0),
        "w_in": w_in,
        "conv_w": nrm(ks[3], (DEPTH, CONV_K, CONV_CH), CONV_K ** -0.5),
        "conv_b": bias(ks[4], CONV_CH),
        "conv_ln_g": gain(ks[5], CONV_CH),
        "conv_ln_b": bias(ks[6], CONV_CH),
        "w_out": nrm(ks[7], (DEPTH, D_MIX, D_MODEL), D_MIX ** -0.5 * DEEPNORM_BETA),
        "ln1_g": gain(ks[8], D_MODEL),
        "ln1_b": bias(ks[9], D_MODEL),
        "mem_wq": nrm(ks[10], (DEPTH, D_MODEL, D_MODEL), D_MODEL ** -0.5),
        "mem_wk": nrm(ks[11], (DEPTH, D_MODEL, D_MODEL), D_MODEL ** -0.5),
        "mem_wv": nrm(ks[12], (DEPTH, D_MODEL, D_MODEL), D_MODEL ** -0.5 * DEEPNORM_BETA),
        "mem_wo": nrm(ks[13], (DEPTH, D_MODEL, D_MODEL), D_MODEL ** -0.5 * DEEPNORM_BETA),
        "ln2_g": gain(ks[14], D_MODEL),
        "ln2_b": bias(ks[15], D_MODEL),
        "ffn_up": nrm(ks[16], (DEPTH, D_MODEL, 2 * D_FF), D_MODEL ** -0.5),
        "ffn_conv_w": nrm(ks[17], (DEPTH, FFN_K, 2 * D_FF), FFN_K ** -0.5),
        "ffn_conv_b": bias(ks[18], 2 * D_FF),
        "ffn_down": nrm(ks[19], (DEPTH, D_FF, D_MODEL), D_FF ** -0.5 * DEEPNORM_BETA),
        "ln3_g": gain(ks[20], D_MODEL),
        "ln3_b": bias(ks[21], D_MODEL),
    }

def reference(x, mem, w_in, conv_w, conv_b, conv_ln_g, conv_ln_b, w_out, ln1_g, ln1_b,
              mem_wq, mem_wk, mem_wv, mem_wo, ln2_g, ln2_b,
              ffn_up, ffn_conv_w, ffn_conv_b, ffn_down, ln3_g, ln3_b):
    for l in range(DEPTH):
        mix = hybrid_mixer(x, w_in[l], conv_w[l], conv_b[l], conv_ln_g[l], conv_ln_b[l], w_out[l])
        x = layer_norm(DEEPNORM_ALPHA * x + mix, ln1_g[l], ln1_b[l])
        cross = memory_cross_attention(x, mem, mem_wq[l], mem_wk[l], mem_wv[l], mem_wo[l])
        x = layer_norm(DEEPNORM_ALPHA * x + cross, ln2_g[l], ln2_b[l])
        ffn = conv_gated_ffn(x, ffn_up[l], ffn_conv_w[l], ffn_conv_b[l], ffn_down[l])
        x = layer_norm(DEEPNORM_ALPHA * x + ffn, ln3_g[l], ln3_b[l])
    return x


_drawn_inputs = setup_inputs


def setup_inputs(seed=0):
    import zlib

    import numpy as np

    out = dict(_drawn_inputs(seed))
    spreads = {}
    factors = {'conv_b': 8.0,
     'conv_ln_g': 4.317,
     'conv_ln_b': 31.294,
     'ln1_b': 5.465,
     'ln2_b': 5.506,
     'ffn_conv_b': 8.0,
     'ln3_b': 5.509}
    for name, (base, spread) in spreads.items():
        noise = np.random.default_rng([zlib.crc32(name.encode()), seed]).standard_normal(out[name].shape)
        drawn = base * np.exp(spread * noise) if base else spread * noise
        out[name] = __import__('jax').numpy.asarray(drawn.astype(out[name].dtype))
    for name, factor in factors.items():
        out[name] = (out[name] * factor).astype(out[name].dtype)
    return out
```

```python
from contextlib import ExitStack

import concourse.bass as bass
from concourse import mybir

F32 = mybir.dt.float32
F32R = mybir.dt.float32r
U8 = mybir.dt.uint8
ALU = mybir.AluOpType
ACT = mybir.ActivationFunctionType
AX = mybir.AxisListType

P = 128
CLAMP = 40.0
NEG = -1.0e30


def decoder_layer(nc, x, mem, w_in, conv_w, conv_b, conv_ln_g, conv_ln_b, w_out, ln1_g, ln1_b,
                  mem_wq, mem_wk, mem_wv, mem_wo, ln2_g, ln2_b,
                  ffn_up, ffn_conv_w, ffn_conv_b, ffn_down, ln3_g, ln3_b, out):
    _, SEQ, D = x.shape
    MEM = mem.shape[1]
    CONV_K, CH = conv_w.shape[1], conv_w.shape[2]
    FK, FF2 = ffn_conv_w.shape[1], ffn_conv_w.shape[2]
    FF = FF2 // 2
    HEADS, HD = 8, (D - CH) // 8
    MHEADS = 4
    MHD = D // MHEADS
    ALPHA = 2.0 ** 0.25
    EPS = 1e-5
    KT = D // P
    TT = SEQ // P
    MT = MEM // P
    CT = CH // P
    FT = FF // P
    H = D // 2
    QOFF, KOFF, VOFF = 2 * CH, 2 * CH + HEADS * HD, 2 * CH + 2 * HEADS * HD
    PAD = CONV_K - 1
    UP = SEQ + PAD

    RING = 4
    AHEAD = RING - 1
    UW = KT * P

    def t_unit(w, c0):
        return w[0, :, c0:c0 + P].rearrange("(k p) n -> p k n", p=P), "t"

    def tok_unit(w, r, c0):
        return w[0, r * 2 * P:(r + 1) * 2 * P, c0:c0 + H].rearrange("(k p) n -> p k n", p=P), "tok"

    units = []
    for c in range(CT):
        units += [t_unit(w_in, CH + c * P), t_unit(w_in, c * P)]
    U_QK = len(units)
    units += [t_unit(w_in, QOFF + i * P) for i in range(2 * HEADS * HD // P)]
    U_V = len(units)
    units += [tok_unit(w_in, r, VOFF) for r in range(KT // 2)]
    U_MK = len(units)
    units += [t_unit(mem_wk, i * P) for i in range(KT)]
    U_OUT = len(units)
    units += [tok_unit(w_out, r, hf * H) for hf in range(2) for r in range(KT // 2)]
    U_MV = len(units)
    units += [tok_unit(mem_wv, r, hf * H) for hf in range(2) for r in range(KT // 2)]
    U_MQ = len(units)
    units += [t_unit(mem_wq, i * P) for i in range(KT)]
    U_MO = len(units)
    units += [tok_unit(mem_wo, r, hf * H) for hf in range(2) for r in range(KT // 2)]
    U_UP = len(units)
    for i in range(FT):
        units += [t_unit(ffn_up, i * P), t_unit(ffn_up, FF + i * P)]
    U_DN = len(units)
    units += [tok_unit(ffn_down, r, hf * H) for hf in range(2) for r in range(FT // 2)]
    NU = len(units)
    DN_HALF = FT // 2

    with ExitStack() as ctx:
        def sem(name):
            return ctx.enter_context(nc.semaphore(name))

        SLAB = 207 * 1024
        SB0 = nc.lookup_mloc(ctx.enter_context(nc.sbuf_tensor("slab", [P, SLAB], U8))).addr
        at_ = [0]

        def place(name, shape, dt=F32, at=None):
            n = 4
            for s in shape[1:]:
                n *= s
            if at is None:
                at = at_[0]
                at_[0] += (n + 63) // 64 * 64
            assert at + n <= SLAB, (name, at, n)
            return nc.alloc_sbuf_tensor_at(name, shape, dt, offset=SB0 + at)

        w_raw = [place(f"w_raw{s}", [P, UW]) for s in range(RING)]
        w_hi = [place(f"w_hi{s}", [P, UW], F32R) for s in range(RING)]
        w_lo = [place(f"w_lo{s}", [P, UW], F32R) for s in range(RING)]
        xres = place("xres", [P, TT, D])
        xt_at = at_[0]
        xt_hi = place("xt_hi", [P, KT, SEQ], F32R)
        xt_lo = place("xt_lo", [P, KT, SEQ], F32R)
        ident = place("ident", [P, P])
        avg = place("avg", [P, P])
        ident_r = place("ident_r", [P, P], F32R)
        negtri_r = place("negtri_r", [P, P], F32R)
        negone_r = place("negone_r", [P, P], F32R)
        hide_r = place("hide_r", [P, P], F32R)
        cw = place("cw", [P, CT, CONV_K])
        cp = place("cp", [P, 3 * CT])
        fp = place("fp", [P, FK + 1, 2 * FT])
        stats = place("stats", [P, TT, 12])
        mv = place("mv", [P, TT, 2])
        vareps = place("vareps", [P, TT])
        lnvar = place("lnvar", [P, TT])
        rstd = place("rstd", [P, TT])
        cmx = place("cmx", [P, MHEADS, TT])
        csum = place("csum", [P, MHEADS, TT])
        crec = place("crec", [P, MHEADS, TT])
        ln_gb = place("ln_gb", [P, 2, D])
        reg = at_[0]
        KB = 1024
        qT = place("qT", [P, HEADS // 2, SEQ], at=reg)
        kT = place("kT", [P, HEADS // 2, SEQ], at=reg + 8 * KB)
        vtok = place("vtok", [P, TT, HEADS * HD], at=reg + 16 * KB)
        mix_hi = place("mix_hi", [P, KT, SEQ], F32R, at=reg + 24 * KB)
        mix_lo = place("mix_lo", [P, KT, SEQ], F32R, at=reg + 40 * KB)
        mt_hi = place("mt_hi", [P, KT, MEM], F32R, at=reg + 56 * KB)
        mt_lo = place("mt_lo", [P, KT, MEM], F32R, at=reg + 64 * KB)
        mkT = place("mkT", [P, KT, MEM], at=reg + 72 * KB)
        memtok = place("memtok", [P, MT, D], at=reg + 72 * KB)
        cacc = place("cacc", [P, CT, SEQ], at=reg + 80 * KB)
        upad = place("upad", [P, CT, UP], at=reg + 88 * KB)
        csq = place("csq", [P, CT, SEQ], at=reg + 88 * KB)
        cw_rows = place("cw_rows", [CONV_K, CH], at=reg + 24 * KB)
        cp_rows = place("cp_rows", [3 * CT, P], at=reg + 27 * KB)
        fp_rows = place("fp_rows", [2 * FT, FK + 1, P], at=reg + 28 * KB)
        negtri = place("negtri", [P, P], at=reg + 44 * KB)
        negone = place("negone", [P, P], at=reg + 45 * KB)
        hide = place("hide", [P, P], at=reg + 46 * KB)
        sig = place("sig", [P, SEQ], at=reg + 40 * KB)
        crstd = place("crstd", [P, SEQ], at=reg + 40 * KB)
        SW = 1280
        E = [place(f"E{i}", [P, SW], at=xt_at + 5 * KB * i) for i in range(2)]
        sp_lo = [place(f"sp_lo{i}", [P, SW], F32R, at=xt_at + 5 * KB * i) for i in range(2)]
        sp_hi = [place(f"sp_hi{i}", [P, SW], F32R, at=xt_at + 5 * KB * (2 + i)) for i in range(2)]
        A = [place(f"A{i}", [P, SW], at=xt_at + 5 * KB * (4 + i)) for i in range(2)]
        mvtok = place("mvtok", [P, MT, D], at=reg)
        mqT = place("mqT", [P, KT, SEQ], at=reg + 8 * KB)
        pr = [place(f"pr{i}", [P, TT, MEM], at=reg + (56 + 4 * i) * KB) for i in range(2)]
        prT = [place(f"prT{i}", [P, MT, SEQ], at=reg + (64 + 4 * i) * KB) for i in range(2)]
        g_hi = place("g_hi", [P, FT, SEQ], F32R, at=reg)
        g_lo = place("g_lo", [P, FT, SEQ], F32R, at=reg + 4 * FT * SEQ)
        f0 = reg + 8 * FT * SEQ
        yv = [place(f"yv{i}", [P, SEQ], at=f0 + 2 * KB * i) for i in range(2)]
        yg = [place(f"yg{i}", [P, SEQ], at=f0 + 2 * KB * (2 + i)) for i in range(2)]

        bank = [ctx.enter_context(nc.psum_tensor(f"bank{i}", [P, SEQ], F32)) for i in range(8)]
        pA = bank[0:2]
        pT = bank[2:6]
        pX = bank[6:8]

        x_loaded = [sem(f"x_loaded{t}") for t in range(TT)]
        mem_loaded = sem("mem_loaded")
        rows_loaded = sem("rows_loaded")
        ln_loaded = sem("ln_loaded")
        raw_loaded = [sem(f"raw_loaded{s}") for s in range(RING)]
        hi_made, lo_made, unit_used = sem("hi_made"), sem("lo_made"), sem("unit_used")
        consts_made, consts_round = sem("consts_made"), sem("consts_round")
        pad_zeroed = sem("pad_zeroed")
        tr_done, tr_hi, tr_lo = sem("tr_done"), sem("tr_hi"), sem("tr_lo")
        rows_turned, params_ready = sem("rows_turned"), sem("params_ready")
        tile_read = [sem("tile_read0"), sem("tile_read1")]
        sig_made, u_made = sem("sig_made"), sem("u_made")
        tap_done = sem("tap_done")
        v_done, v_read = sem("v_done"), sem("v_read")
        z_done, clamp_made, exp_made, ln_made = sem("z_done"), sem("clamp_made"), sem("exp_made"), sem("ln_made")
        sp_made, sphi_made, splo_made = sem("sp_made"), sem("sphi_made"), sem("splo_made")
        s_done, a_made = sem("s_done"), sem("a_made")
        pv_done, pv_hi, pv_lo = sem("pv_done"), sem("pv_hi"), sem("pv_lo")
        cmean_done, ccent_made, csq_made = sem("cmean_done"), sem("ccent_made"), sem("csq_made")
        cvar_done, cln_made, crstd_made = sem("cvar_done"), sem("cln_made"), sem("crstd_made")
        cnorm_made, cact_made, chi_made, clo_made = sem("cnorm_made"), sem("cact_made"), sem("chi_made"), sem("clo_made")
        cve_made = sem("cve_made")
        tok_done, tok_read = sem("tok_done"), sem("tok_read")
        st_made, ag_made, ve_made, lv_made, rs_made = sem("st_made"), sem("ag_made"), sem("ve_made"), sem("lv_made"), sem("rs_made")
        gain_made, ln_made2 = sem("gain_made"), sem("ln_done")
        mv_read = sem("mv_read")
        cs_done, cmax_made, cexp_made = sem("cs_done"), sem("cmax_made"), sem("cexp_made")
        crec_made, cp_made = sem("crec_made"), sem("cprob_made")
        ct_done, ct_read0, ct_read1 = sem("ct_done"), sem("ct_read0"), sem("ct_read1")
        co_done, co_hi, co_lo = sem("co_done"), sem("co_hi"), sem("co_lo")
        yv_made, yg_made = sem("yv_made"), sem("yg_made")
        tv1, tg1, tv2, tg2 = sem("tapv1"), sem("tapg1"), sem("tapv2"), sem("tapg2")
        silu_made, gm_made, ghi_made, glo_made = sem("silu_made"), sem("gm_made"), sem("ghi_made"), sem("glo_made")
        stored = sem("stored")

        J_QK, J_MK, J_MQ = 0, 2 * TT, 2 * TT + KT
        G_MEM, G_LN1, G_LN2 = 2 * TT, 2 * TT + 2 * MT, 4 * TT + 2 * MT

        SEG = {0: (0, 0, 0), 1: (1, 0, 512), 3: (1, 384, 896), 2: (2, 0, 1024)}
        BANKW = [(0, 512), (512, 512), (1024, 256)]

        def zbank(h, b):
            return (pT[0], pT[1], pX[0])[b] if h % 2 == 0 else (pT[2], pT[3], pX[1])[b]

        HALF_END = [U_OUT + RING, U_OUT + 2 * RING, U_MO + RING, U_MO + 2 * RING, U_DN + DN_HALF, U_DN + 2 * DN_HALF]

        def tok_bank(layer, t):
            return bank[4 + t] if layer == 2 else pT[t]

        block = ctx.enter_context(nc.Block())

        @block.sync
        def _(sp):
            def load_unit(u):
                s = u % RING
                if u >= RING:
                    sp.wait_ge(lo_made, u - RING + 1)
                src, _ = units[u]
                k = src.shape[1]
                sp.dma_start(w_raw[s][:, :].rearrange("p (k n) -> p k n", k=k), src).then_inc(raw_loaded[s], 16)

            def load_ln(g, b):
                for i, v in enumerate((g, b)):
                    sp.dma_start(ln_gb[:, i, :], v[0:1, :].broadcast_to([P, D])).then_inc(ln_loaded, 16)

            for t in range(TT):
                sp.dma_start(xres[:, t, :], x[0, t * P:(t + 1) * P, :]).then_inc(x_loaded[t], 16)
            for u in range(NU):
                load_unit(u)
                if u == U_V:
                    load_ln(ln1_g, ln1_b)
                if u == U_MO:
                    sp.wait_ge(ln_made2, TT)
                    load_ln(ln2_g, ln2_b)
                if u == U_DN:
                    sp.wait_ge(ln_made2, 2 * TT)
                    load_ln(ln3_g, ln3_b)
            for t in range(TT):
                sp.wait_ge(ln_made2, 2 * TT + t + 1)
                sp.dma_start(out[0, t * P:(t + 1) * P, :], xres[:, t, :]).then_inc(stored, 16)
            sp.wait_ge(stored, 16 * TT)

        @block.gpsimd
        def _(pool):
            nc.gpsimd.memset(ident[:, :], 0.0).then_inc(consts_made, 1)
            nc.gpsimd.memset(negtri[:, :], -1.0).then_inc(consts_made, 1)
            nc.gpsimd.memset(negone[:, :], -1.0).then_inc(consts_made, 1)
            nc.gpsimd.memset(hide[:, :], 0.0).then_inc(consts_made, 1)
            nc.gpsimd.memset(avg[:, :], 1.0 / CH).then_inc(consts_made, 1)
            pool.wait_ge(consts_made, 5)
            nc.gpsimd.affine_select(out=ident[:, :], in_=ident[:, :], compare_op=ALU.not_equal, fill=1.0, base=0,
                                    pattern=[[-1, P]], channel_multiplier=1).then_inc(consts_made, 1)
            nc.gpsimd.affine_select(out=negtri[:, :], in_=negtri[:, :], compare_op=ALU.is_ge, fill=0.0, base=0,
                                    pattern=[[-1, P]], channel_multiplier=1).then_inc(consts_made, 1)
            nc.gpsimd.affine_select(out=hide[:, :], in_=hide[:, :], compare_op=ALU.is_gt, fill=NEG, base=0,
                                    pattern=[[1, P]], channel_multiplier=-1).then_inc(consts_made, 1)
            nc.gpsimd.memset(upad[:, :, 0:PAD], 0.0).then_inc(pad_zeroed, 1)

        @block.scalar
        def _(act):
            def convert(u):
                if u >= NU:
                    return
                s = u % RING
                act.wait_ge(raw_loaded[s], 16 * (u // RING + 1))
                if u >= RING:
                    act.wait_ge(unit_used, u - RING + 1)
                nc.scalar.copy(w_hi[s][:, :], w_raw[s][:, :]).then_inc(hi_made, 1)

            def turn_hi(g, dst, t):
                act.wait_ge(tr_done, g + 1)
                nc.scalar.copy(dst[:, 4 * (g % 2):4 * (g % 2) + 4, t * P:(t + 1) * P],
                               pX[g % 2][:, :].rearrange("p (k n) -> p k n", k=4)).then_inc(tr_hi, 1)

            def tile(u, j, dst, scale=1.0):
                act.wait_ge(unit_used, u + 1)
                n = dst.shape[1]
                nc.scalar.activation(dst, pA[j % 2][:, 0:n], ACT.Copy, scale=scale).then_inc(tile_read[j % 2], 1)

            act.dma_start(cw_rows[:, :], conv_w[0]).then_inc(rows_loaded, 16)
            for i, v in enumerate((conv_b, conv_ln_g, conv_ln_b)):
                act.dma_start(cp_rows[i * CT:(i + 1) * CT, :], v[0].rearrange("(c p) -> c p", p=P)).then_inc(rows_loaded, 16)
            for i in range(FK):
                act.dma_start(fp_rows[:, i, :], ffn_conv_w[0, i].rearrange("(c p) -> c p", p=P)).then_inc(rows_loaded, 16)
            act.dma_start(fp_rows[:, FK, :], ffn_conv_b[0].rearrange("(c p) -> c p", p=P)).then_inc(rows_loaded, 16)
            act.dma_start(memtok[:, :, :], mem[0].rearrange("(t p) d -> p t d", p=P)).then_inc(mem_loaded, 16)
            act.wait_ge(consts_made, 8)
            for dst, src in ((ident_r, ident), (negtri_r, negtri), (negone_r, negone), (hide_r, hide)):
                nc.scalar.copy(dst[:, :], src[:, :]).then_inc(consts_round, 1)
            for t in range(TT):
                for hf in range(2):
                    turn_hi(2 * t + hf, xt_hi, t)
            for u in range(AHEAD):
                convert(u)
            act.wait_ge(rows_turned, 1)
            nc.scalar.copy(cw[:, :, :], pT[0][:, 0:CT * CONV_K].rearrange("p (c k) -> p c k", c=CT)).then_inc(params_ready, 1)
            nc.scalar.copy(cp[:, :], pT[1][:, 0:3 * CT]).then_inc(params_ready, 1)
            nc.scalar.copy(fp[:, :, :], pT[2][:, 0:(FK + 1) * 2 * FT].rearrange("p (k c) -> p k c", k=FK + 1)).then_inc(params_ready, 1)
            for c in range(CT):
                convert(2 * c + AHEAD)
                act.wait_ge(unit_used, 2 * c + 1)
                if c:
                    act.wait_ge(u_made, c)
                nc.scalar.activation(sig[:, :], pA[0][:, :], ACT.Sigmoid).then_inc(sig_made, 1)
                convert(2 * c + 1 + AHEAD)
            for t in range(MT):
                for hf in range(2):
                    turn_hi(G_MEM + 2 * t + hf, mt_hi, t)
            for i in range(8):
                convert(U_QK + i + AHEAD)
                dst = (qT if i < 4 else kT)[:, i % 4, :]
                tile(U_QK + i, J_QK + i, dst, HD ** -0.5 if i < 4 else 1.0)
            convert(U_V + AHEAD)
            for t in range(TT):
                if t == TT - 1:
                    for u in range(3):
                        convert(U_V + RING + u)
                if t < TT - 1:
                    act.wait_ge(v_done, t + 1)
                else:
                    act.wait_ge(unit_used, U_V + RING)
                nc.scalar.copy(vtok[:, t, :], pT[t][:, :]).then_inc(v_read, 1)
            for i in range(KT):
                convert(U_MK + i + AHEAD)
                tile(U_MK + i, J_MK + i, mkT[:, i, :])

            nc.scalar.preload_act_table_set("natural_log_exp_and_others")

            def softplus_parts(h):
                for b, (c0, w) in enumerate(BANKW):
                    act.wait_ge(clamp_made, 3 * h + b + 1)
                    e = E[h % 2][:, c0:c0 + w]
                    nc.scalar.activation(e, e, ACT.Exp).then_inc(exp_made, 1)
                for b, (c0, w) in enumerate(BANKW):
                    act.wait_ge(exp_made, 3 * h + b + 1)
                    e = E[h % 2][:, c0:c0 + w]
                    nc.scalar.activation(e, e, ACT.Ln, bias=1.0).then_inc(ln_made, 1)

            def weights_of(h):
                for b, (c0, w) in enumerate(BANKW):
                    act.wait_ge(s_done, 3 * h + b + 1)
                    nc.scalar.activation(A[h % 2][:, c0:c0 + w], zbank(h, b)[:, 0:w], ACT.Exp).then_inc(a_made, 1)

            def head_out_hi(h):
                act.wait_ge(pv_done, h + 1)
                p0 = HD * (h % 2)
                nc.scalar.copy(mix_hi[p0:p0 + HD, CT + h // 2, :], pA[0][p0:p0 + HD, :]).then_inc(pv_hi, 1)

            softplus_parts(0)
            softplus_parts(1)
            for h in range(HEADS):
                weights_of(h)
                if h:
                    head_out_hi(h - 1)
                if h == 2:
                    for c in range(CT):
                        act.wait_ge(ccent_made, c + 1)
                        nc.scalar.activation(csq[:, c, :], cacc[:, c, :], ACT.Square).then_inc(csq_made, 1)
                if h == 4:
                    act.wait_ge(cve_made, 1)
                    nc.scalar.activation(crstd[:, :], crstd[:, :], ACT.Ln).then_inc(cln_made, 1)
                    act.wait_ge(cln_made, 1)
                    nc.scalar.activation(crstd[:, :], crstd[:, :], ACT.Exp, scale=-0.5).then_inc(crstd_made, 1)
                if h + 2 < HEADS:
                    softplus_parts(h + 2)
                if h == 5:
                    for c in range(CT):
                        act.wait_ge(cnorm_made, c + 1)
                        nc.scalar.activation(cacc[:, c, :], cacc[:, c, :], ACT.Silu, scale=cp[:, CT + c:CT + c + 1],
                                             bias=cp[:, 2 * CT + c:2 * CT + c + 1]).then_inc(cact_made, 1)
                    for c in range(CT):
                        act.wait_ge(cact_made, c + 1)
                        nc.scalar.copy(mix_hi[:, c, :], cacc[:, c, :]).then_inc(chi_made, 1)
                    nc.scalar.preload_act_table_set("natural_log_exp_and_others")
            head_out_hi(HEADS - 1)

            def ln_rstd(n):
                t = n % TT
                act.wait_ge(ve_made, n + 1)
                nc.scalar.activation(lnvar[:, t:t + 1], vareps[:, t:t + 1], ACT.Ln).then_inc(lv_made, 1)
                act.wait_ge(lv_made, n + 1)
                nc.scalar.activation(rstd[:, t:t + 1], lnvar[:, t:t + 1], ACT.Exp, scale=-0.5).then_inc(rs_made, 1)

            def turn2(g0, t):
                turn_hi(g0 + 2 * t, xt_hi, t)
                turn_hi(g0 + 2 * t + 1, xt_hi, t)

            def mem_values(hf):
                act.wait_ge(unit_used, U_MV + (hf + 1) * RING)
                for m in range(MT):
                    nc.scalar.copy(mvtok[:, m, hf * H:(hf + 1) * H], pA[m][:, :]).then_inc(mv_read, 1)

            convert(U_OUT + AHEAD)
            for u in range(4):
                convert(U_OUT + RING + u)
            ln_rstd(0)
            ln_rstd(1)
            turn2(G_LN1, 0)
            ln_rstd(2)
            for u in range(3):
                convert(U_MV + u)
            turn2(G_LN1, 1)
            ln_rstd(3)
            turn2(G_LN1, 2)
            for u in range(3, 7):
                convert(U_MV + u)
            mem_values(0)
            turn2(G_LN1, 3)
            for u in range(7, 11):
                convert(U_MV + u)
            mem_values(1)
            for i in range(KT):
                convert(U_MQ + i + AHEAD)
                tile(U_MQ + i, J_MQ + i, mqT[:, i, :], MHD ** -0.5)

            def cross_exp(h):
                act.wait_ge(cmax_made, h + 1)
                if h >= 2:
                    act.wait_ge(ct_done, MT * (h - 1))
                for t in range(TT):
                    nc.scalar.activation(pr[h % 2][:, t, :], pT[2 * (h % 2) + t // 2][:, MEM * (t % 2):MEM * (t % 2) + MEM],
                                         ACT.Exp, bias=cmx[:, h, t:t + 1],
                                         accum_out=csum[:, h, t:t + 1]).then_inc(cexp_made, 1)

            def cross_turn0(h):
                act.wait_ge(ct_done, MT * h + 1)
                if h >= 2:
                    act.wait_ge(co_done, 2 * (h - 1))
                nc.scalar.copy(prT[h % 2][:, 0, :], pX[0][:, :]).then_inc(ct_read0, 1)

            def cross_out_hi(h):
                for d in range(2):
                    act.wait_ge(co_done, 2 * h + d + 1)
                    nc.scalar.copy(mix_hi[:, 2 * h + d, :], pA[d][:, :]).then_inc(co_hi, 1)

            cross_exp(0)
            for h in range(MHEADS):
                if h + 1 < MHEADS:
                    cross_exp(h + 1)
                cross_turn0(h)
                cross_out_hi(h)

            convert(U_MO + AHEAD)
            for u in range(4):
                convert(U_MO + RING + u)
            ln_rstd(TT + 0)
            ln_rstd(TT + 1)
            turn2(G_LN2, 0)
            ln_rstd(TT + 2)
            for u in range(3):
                convert(U_UP + u)
            turn2(G_LN2, 1)
            ln_rstd(TT + 3)
            turn2(G_LN2, 2)
            turn2(G_LN2, 3)

            def ffn_silu(i):
                act.wait_ge(tg2, i + 1)
                nc.scalar.activation(yg[i % 2][:, :], yg[i % 2][:, :], ACT.Silu).then_inc(silu_made, 1)

            for i in range(FT):
                convert(U_UP + 2 * i + AHEAD)
                if i >= 2:
                    act.wait_ge(glo_made, i - 1)
                act.wait_ge(unit_used, U_UP + 2 * i + 1)
                nc.scalar.activation(yv[i % 2][:, :], bank[2 * (i % 2)][:, :], ACT.Identity,
                                     scale=fp[:, FK - 1, i:i + 1], bias=fp[:, FK, i:i + 1]).then_inc(yv_made, 1)
                convert(U_UP + 2 * i + 1 + AHEAD)
                act.wait_ge(unit_used, U_UP + 2 * i + 2)
                nc.scalar.activation(yg[i % 2][:, :], bank[2 * (i % 2) + 1][:, :], ACT.Identity,
                                     scale=fp[:, FK - 1, FT + i:FT + i + 1], bias=fp[:, FK, FT + i:FT + i + 1]).then_inc(yg_made, 1)
                if i:
                    ffn_silu(i - 1)
            ffn_silu(FT - 1)
            nc.scalar.preload_act_table_set("natural_log_exp_and_others")
            for u in range(U_DN + AHEAD, NU):
                convert(u)
            for t in range(TT):
                ln_rstd(2 * TT + t)

        @block.vector
        def _(dve):
            def convert(u):
                if u >= NU:
                    return
                s = u % RING
                dve.wait_ge(hi_made, u + 1)
                nc.vector.tensor_tensor(w_lo[s][:, :], w_raw[s][:, :], w_hi[s][:, :].bitcast(F32),
                                        ALU.subtract).then_inc(lo_made, 1)

            def turn_lo(g, hi, lo, t):
                dve.wait_ge(tr_hi, g + 1)
                k0 = 4 * (g % 2)
                nc.vector.tensor_tensor(lo[:, k0:k0 + 4, t * P:(t + 1) * P],
                                        pX[g % 2][:, :].rearrange("p (k n) -> p k n", k=4),
                                        hi[:, k0:k0 + 4, t * P:(t + 1) * P].bitcast(F32), ALU.subtract).then_inc(tr_lo, 1)

            taps = [(c, j) for c in range(CT) for j in range(CONV_K)]
            at = [0]

            def conv_taps(n):
                for c, j in taps[at[0]:at[0] + n]:
                    dve.wait_ge(u_made, c + 1)
                    y, u, w = cacc[:, c, :], upad[:, c, j:j + SEQ], cw[:, c, j:j + 1]
                    if at[0]:
                        dve.wait_ge(tap_done, at[0])
                    if j == 0:
                        nc.vector.tensor_scalar(y, u, w, cp[:, c:c + 1], ALU.mult, ALU.add).then_inc(tap_done, 1)
                    else:
                        nc.vector.scalar_tensor_tensor(y, u, w, y, ALU.mult, ALU.add).then_inc(tap_done, 1)
                    at[0] += 1

            for t in range(TT):
                for hf in range(2):
                    turn_lo(2 * t + hf, xt_hi, xt_lo, t)
            for u in range(AHEAD):
                convert(u)
            dve.wait_ge(params_ready, 3)
            dve.wait_ge(pad_zeroed, 1)
            for c in range(CT):
                convert(2 * c + AHEAD)
                if c:
                    conv_taps(5)
                convert(2 * c + 1 + AHEAD)
                dve.wait_ge(unit_used, 2 * c + 2)
                dve.wait_ge(sig_made, c + 1)
                nc.vector.tensor_tensor(upad[:, c, PAD:UP], pA[1][:, :], sig[:, :], ALU.mult).then_inc(u_made, 1)
                conv_taps(5)
            for t in range(MT):
                for hf in range(2):
                    turn_lo(G_MEM + 2 * t + hf, mt_hi, mt_lo, t)
            for i in range(8):
                convert(U_QK + i + AHEAD)
                conv_taps(5)
            convert(U_V + AHEAD)
            conv_taps(15)
            for u in range(3):
                convert(U_V + RING + u)
            for i in range(KT):
                convert(U_MK + i + AHEAD)
                conv_taps(4 if i < KT - 1 else len(taps))

            def scores_clamp(h):
                for b, (c0, w) in enumerate(BANKW):
                    dve.wait_ge(z_done, 3 * h + b + 1)
                    nc.vector.tensor_scalar(E[h % 2][:, c0:c0 + w], zbank(h, b)[:, 0:w], CLAMP, None,
                                            ALU.min).then_inc(clamp_made, 1)

            def softplus(h):
                for b, (c0, w) in enumerate(BANKW):
                    dve.wait_ge(ln_made, 3 * h + b + 1)
                    e = E[h % 2][:, c0:c0 + w]
                    nc.vector.tensor_tensor(e, zbank(h, b)[:, 0:w], e, ALU.max).then_inc(sp_made, 1)
                for b, (c0, w) in enumerate(BANKW):
                    dve.wait_ge(sp_made, 3 * h + b + 1)
                    nc.vector.tensor_copy(sp_hi[h % 2][:, c0:c0 + w], E[h % 2][:, c0:c0 + w]).then_inc(sphi_made, 1)
                for b, (c0, w) in enumerate(BANKW):
                    dve.wait_ge(sphi_made, 3 * h + b + 1)
                    nc.vector.tensor_tensor(sp_lo[h % 2][:, c0:c0 + w], E[h % 2][:, c0:c0 + w],
                                            sp_hi[h % 2][:, c0:c0 + w].bitcast(F32), ALU.subtract).then_inc(splo_made, 1)

            def head_out_lo(h):
                dve.wait_ge(pv_hi, h + 1)
                p0 = HD * (h % 2)
                nc.vector.tensor_tensor(mix_lo[p0:p0 + HD, CT + h // 2, :], pA[0][p0:p0 + HD, :],
                                        mix_hi[p0:p0 + HD, CT + h // 2, :].bitcast(F32), ALU.subtract).then_inc(pv_lo, 1)

            scores_clamp(0)
            softplus(0)
            scores_clamp(1)
            softplus(1)
            for h in range(HEADS):
                if h:
                    head_out_lo(h - 1)
                if h + 2 < HEADS:
                    scores_clamp(h + 2)
                if h == 1:
                    dve.wait_ge(cmean_done, 1)
                    for c in range(CT):
                        nc.vector.tensor_tensor(cacc[:, c, :], cacc[:, c, :], pA[1][:, :], ALU.subtract).then_inc(ccent_made, 1)
                if h == 3:
                    dve.wait_ge(cvar_done, 1)
                    nc.vector.tensor_scalar(crstd[:, :], pA[1][:, :], EPS, None, ALU.add).then_inc(cve_made, 1)
                if h == 4:
                    dve.wait_ge(crstd_made, 1)
                    for c in range(CT):
                        nc.vector.tensor_tensor(cacc[:, c, :], cacc[:, c, :], crstd[:, :], ALU.mult).then_inc(cnorm_made, 1)
                if h == 6:
                    for c in range(CT):
                        dve.wait_ge(chi_made, c + 1)
                        nc.vector.tensor_tensor(mix_lo[:, c, :], cacc[:, c, :], mix_hi[:, c, :].bitcast(F32),
                                                ALU.subtract).then_inc(clo_made, 1)
                if h + 2 < HEADS:
                    softplus(h + 2)
            head_out_lo(HEADS - 1)

            def residual(n, hf):
                t = n % TT
                half = 2 * (n // TT) + hf
                idx = half * TT + t
                if t < TT - 1:
                    dve.wait_ge(tok_done, (TT - 1) * half + t + 1)
                else:
                    dve.wait_ge(unit_used, HALF_END[half])
                xs = xres[:, t, hf * H:(hf + 1) * H]
                nc.vector.scalar_tensor_tensor(xs, xs, ALPHA, tok_bank(n // TT, t)[:, :], ALU.mult, ALU.add).then_inc(tok_read, 1)
                dve.wait_ge(tok_read, idx + 1)
                nc.vector.bn_stats(stats[:, t, 6 * hf:6 * hf + 6], xs).then_inc(st_made, 1)
                return idx

            def layer_norm(n):
                t = n % TT
                idx = residual(n, 1)
                dve.wait_ge(st_made, idx + 1)
                nc.vector.bn_aggr(mv[:, t, :], stats[:, t, :]).then_inc(ag_made, 1)
                dve.wait_ge(ag_made, n + 1)
                nc.vector.tensor_scalar(vareps[:, t:t + 1], mv[:, t, 1:2], EPS, None, ALU.add).then_inc(ve_made, 1)
                if t == 0:
                    dve.wait_ge(ln_loaded, 32 * (n // TT + 1))
                nc.vector.scalar_tensor_tensor(xres[:, t, :], xres[:, t, :], mv[:, t, 0:1], ln_gb[:, 0, :],
                                               ALU.subtract, ALU.mult).then_inc(gain_made, 1)
                dve.wait_ge(gain_made, n + 1)
                dve.wait_ge(rs_made, n + 1)
                nc.vector.scalar_tensor_tensor(xres[:, t, :], xres[:, t, :], rstd[:, t:t + 1], ln_gb[:, 1, :],
                                               ALU.mult, ALU.add).then_inc(ln_made2, 1)

            def turn2(g0, t):
                turn_lo(g0 + 2 * t, xt_hi, xt_lo, t)
                turn_lo(g0 + 2 * t + 1, xt_hi, xt_lo, t)

            convert(U_OUT + AHEAD)
            for t in range(TT - 1):
                residual(t, 0)
            for u in range(3):
                convert(U_OUT + RING + u)
            residual(TT - 1, 0)
            convert(U_OUT + RING + 3)
            layer_norm(0)
            layer_norm(1)
            turn2(G_LN1, 0)
            layer_norm(2)
            for u in range(3):
                convert(U_MV + u)
            turn2(G_LN1, 1)
            layer_norm(3)
            turn2(G_LN1, 2)
            for u in range(3, 7):
                convert(U_MV + u)
            turn2(G_LN1, 3)
            for u in range(7, 11):
                convert(U_MV + u)
            for i in range(KT):
                convert(U_MQ + i + AHEAD)

            def cross_max(h):
                for i in range(2):
                    dve.wait_ge(cs_done, 2 * h + i + 1)
                    ins = nc.vector.tensor_reduce(cmx[:, h, 2 * i:2 * i + 2],
                                                  pT[2 * (h % 2) + i][:, :].rearrange("p (t m) -> p t m", t=2),
                                                  AX.X, ALU.max, negate=True)
                ins.then_inc(cmax_made, 1)

            def cross_norm(h):
                dve.wait_ge(cexp_made, TT * (h + 1))
                nc.vector.reciprocal(crec[:, h, :], csum[:, h, :]).then_inc(crec_made, 1)
                dve.wait_ge(crec_made, h + 1)
                for t in range(TT):
                    nc.vector.tensor_scalar(pr[h % 2][:, t, :], pr[h % 2][:, t, :], crec[:, h, t:t + 1], None,
                                            ALU.mult).then_inc(cp_made, 1)

            def cross_turn1(h):
                dve.wait_ge(ct_done, MT * h + 2)
                if h >= 2:
                    dve.wait_ge(co_done, 2 * (h - 1))
                nc.vector.tensor_copy(prT[h % 2][:, 1, :], pX[1][:, :]).then_inc(ct_read1, 1)

            def cross_out_lo(h):
                for d in range(2):
                    dve.wait_ge(co_hi, 2 * h + d + 1)
                    nc.vector.tensor_tensor(mix_lo[:, 2 * h + d, :], pA[d][:, :], mix_hi[:, 2 * h + d, :].bitcast(F32),
                                            ALU.subtract).then_inc(co_lo, 1)

            cross_max(0)
            cross_norm(0)
            for h in range(MHEADS):
                if h + 1 < MHEADS:
                    cross_max(h + 1)
                    cross_norm(h + 1)
                cross_turn1(h)
                cross_out_lo(h)

            convert(U_MO + AHEAD)
            for t in range(TT - 1):
                residual(TT + t, 0)
            for u in range(3):
                convert(U_MO + RING + u)
            residual(2 * TT - 1, 0)
            convert(U_MO + RING + 3)
            layer_norm(TT + 0)
            layer_norm(TT + 1)
            turn2(G_LN2, 0)
            layer_norm(TT + 2)
            for u in range(3):
                convert(U_UP + u)
            turn2(G_LN2, 1)
            layer_norm(TT + 3)
            turn2(G_LN2, 2)
            turn2(G_LN2, 3)

            def ffn_tap(y, ps, tap, col, ready, n, signal):
                back = FK - 1 - tap
                dve.wait_ge(ready, n + 1)
                nc.vector.scalar_tensor_tensor(y[:, back:SEQ], ps[:, 0:SEQ - back], fp[:, tap, col:col + 1],
                                               y[:, back:SEQ], ALU.mult, ALU.add).then_inc(signal, 1)

            def ffn_gate(i):
                b = i % 2
                dve.wait_ge(silu_made, i + 1)
                nc.vector.tensor_tensor(yv[b][:, :], yv[b][:, :], yg[b][:, :], ALU.mult).then_inc(gm_made, 1)
                dve.wait_ge(gm_made, i + 1)
                nc.vector.tensor_copy(g_hi[:, i, :], yv[b][:, :]).then_inc(ghi_made, 1)
                dve.wait_ge(ghi_made, i + 1)
                nc.vector.tensor_tensor(g_lo[:, i, :], yv[b][:, :], g_hi[:, i, :].bitcast(F32),
                                        ALU.subtract).then_inc(glo_made, 1)

            for i in range(FT):
                b = i % 2
                convert(U_UP + 2 * i + AHEAD)
                ffn_tap(yv[b], bank[2 * b], 1, i, yv_made, i, tv1)
                convert(U_UP + 2 * i + 1 + AHEAD)
                ffn_tap(yg[b], bank[2 * b + 1], 1, FT + i, yg_made, i, tg1)
                ffn_tap(yv[b], bank[2 * b], 0, i, tv1, i, tv2)
                ffn_tap(yg[b], bank[2 * b + 1], 0, FT + i, tg1, i, tg2)
                if i:
                    ffn_gate(i - 1)
            ffn_gate(FT - 1)

            last = DN_HALF % RING
            for u in range(U_DN + AHEAD, U_DN + DN_HALF + RING - last):
                convert(u)
            for t in range(TT - 1):
                residual(2 * TT + t, 0)
            for u in range(U_DN + DN_HALF + RING - last, U_DN + DN_HALF + RING - 1):
                convert(u)
            residual(3 * TT - 1, 0)
            for u in range(U_DN + DN_HALF + RING - 1, NU):
                convert(u)
            for t in range(TT):
                layer_norm(2 * TT + t)

        @block.tensor
        def _(pe):
            def turn(g, src, dst_free_wait=True):
                if g >= 2:
                    pe.wait_ge(tr_lo, g - 1)
                for k in range(4):
                    c0 = (4 * (g % 2) + k) * P
                    ins = nc.tensor.transpose(pX[g % 2][:, k * P:(k + 1) * P], src[:, c0:c0 + P], ident[:, :])
                ins.then_inc(tr_done, 1)

            def turn2(g0, t, n):
                pe.wait_ge(ln_made2, n + 1)
                turn(g0 + 2 * t, xres[:, t, :])
                turn(g0 + 2 * t + 1, xres[:, t, :])

            def t_tile(u, dst, hi, lo):
                s = u % RING
                pe.wait_ge(lo_made, u + 1)
                for k in range(KT):
                    wh, wl = w_hi[s][:, k * P:(k + 1) * P], w_lo[s][:, k * P:(k + 1) * P]
                    nc.tensor.matmul(dst, wh, hi[:, k, :], start=(k == 0), stop=False)
                    nc.tensor.matmul(dst, wh, lo[:, k, :], start=False, stop=False)
                    ins = nc.tensor.matmul(dst, wl, hi[:, k, :], start=False, stop=(k == KT - 1))
                return ins

            def t_proj(u, j, hi, lo, n=SEQ):
                if j >= 2:
                    pe.wait_ge(tile_read[j % 2], j // 2)
                t_tile(u, pA[j % 2][:, 0:n], hi, lo).then_inc(unit_used, 1)

            def tok_part(u, dst, hi, lo, t, k0, first, last):
                s = u % RING
                pe.wait_ge(lo_made, u + 1)
                for kk in range(2):
                    xh, xl = hi[:, k0 + kk, t * P:(t + 1) * P], lo[:, k0 + kk, t * P:(t + 1) * P]
                    wh, wl = w_hi[s][:, kk * H:(kk + 1) * H], w_lo[s][:, kk * H:(kk + 1) * H]
                    nc.tensor.matmul(dst, xh, wh, start=(first and kk == 0), stop=False)
                    nc.tensor.matmul(dst, xh, wl, start=False, stop=False)
                    ins = nc.tensor.matmul(dst, xl, wh, start=False, stop=(last and kk == 1))
                return ins

            def tok_tile(u0, n, t, dst, hi, lo, k0, first, last, done):
                for r in range(n):
                    ins = tok_part(u0 + r, dst, hi, lo, t, k0 + 2 * r, first and r == 0, last and r == n - 1)
                    if t == TT - 1:
                        ins.then_inc(unit_used, 1)
                if t < TT - 1 and last:
                    ins.then_inc(done, 1)

            def tok_half(u0, half, t, hi, lo):
                if half % 2:
                    pe.wait_ge(tok_read, TT * (half - 1) + t + 1)
                tok_tile(u0, RING, t, pT[t][:, :], hi, lo, 0, True, True, tok_done)

            pe.wait_ge(consts_made, 8)
            for t in range(TT):
                pe.wait_ge(x_loaded[t], 16)
                turn(2 * t, xres[:, t, :])
                turn(2 * t + 1, xres[:, t, :])
            pe.wait_ge(rows_loaded, 16 * (FK + 5))
            for c in range(CT):
                nc.tensor.transpose(pT[0][:, c * CONV_K:(c + 1) * CONV_K], cw_rows[:, c * P:(c + 1) * P],
                                    ident[0:CONV_K, 0:CONV_K])
            nc.tensor.transpose(pT[1][:, 0:3 * CT], cp_rows[:, :], ident[0:3 * CT, 0:3 * CT])
            for k in range(FK + 1):
                ins = nc.tensor.transpose(pT[2][:, k * 2 * FT:(k + 1) * 2 * FT], fp_rows[:, k, :],
                                          ident[0:2 * FT, 0:2 * FT])
            ins.then_inc(rows_turned, 1)
            pe.wait_ge(tr_lo, 2 * TT)
            for c in range(CT):
                if c:
                    pe.wait_ge(sig_made, c)
                t_tile(2 * c, pA[0][:, :], xt_hi, xt_lo).then_inc(unit_used, 1)
                if c:
                    pe.wait_ge(u_made, c)
                t_tile(2 * c + 1, pA[1][:, :], xt_hi, xt_lo).then_inc(unit_used, 1)
            pe.wait_ge(mem_loaded, 16)
            for t in range(MT):
                turn(G_MEM + 2 * t, memtok[:, t, :])
                turn(G_MEM + 2 * t + 1, memtok[:, t, :])
            for i in range(2 * TT):
                if i < 2:
                    pe.wait_ge((sig_made, u_made)[i], CT)
                t_proj(U_QK + i, J_QK + i, xt_hi, xt_lo)
            pe.wait_ge(params_ready, 3)
            for t in range(TT):
                tok_tile(U_V, RING, t, pT[t][:, :], xt_hi, xt_lo, 0, True, True, v_done)
            pe.wait_ge(tr_lo, G_LN1)
            for i in range(KT):
                t_proj(U_MK + i, J_MK + i, mt_hi, mt_lo, MEM)

            def scores(h):
                p0 = HD * (h % 2)
                for j in (0, 1, 3, 2):
                    b, c0, _ = SEG[j]
                    n = SEQ - j * P
                    nc.tensor.matmul(zbank(h, b)[:, c0:c0 + n], kT[p0:p0 + HD, h // 2, j * P:(j + 1) * P],
                                     qT[p0:p0 + HD, h // 2, j * P:SEQ], start=(j != 3), stop=False,
                                     skip_group_check=True)
                for j in (0, 1, 3, 2):
                    b, c0, _ = SEG[j]
                    ins = nc.tensor.matmul(zbank(h, b)[:, c0:c0 + P], ident_r[:, :], hide_r[:, :], start=False,
                                           stop=True, skip_group_check=True)
                    if j != 1:
                        ins.then_inc(z_done, 1)

            def sums(h):
                pe.wait_ge(splo_made, 3 * (h + 1))
                for j in (0, 1, 3, 2):
                    b, c0, _ = SEG[j]
                    for jj in range(j, TT):
                        s0, n = SEG[jj][2], SEQ - jj * P
                        w = negtri_r if jj == j else negone_r
                        o = zbank(h, b)[:, c0 + (jj - j) * P:c0 + (jj - j) * P + n]
                        nc.tensor.matmul(o, w[:, :], sp_hi[h % 2][:, s0:s0 + n], start=False, stop=False,
                                         skip_group_check=True)
                        ins = nc.tensor.matmul(o, w[:, :], sp_lo[h % 2][:, s0:s0 + n], start=False, stop=True,
                                               skip_group_check=True)
                    if j != 1:
                        ins.then_inc(s_done, 1)

            def head_out(h):
                pe.wait_ge(a_made, 3 * (h + 1))
                if h:
                    pe.wait_ge(pv_lo, h)
                p0 = HD * (h % 2)
                for j in range(TT):
                    s0, n = SEG[j][2], SEQ - j * P
                    ins = nc.tensor.matmul(pA[0][p0:p0 + HD, j * P:SEQ], vtok[:, j, h * HD:(h + 1) * HD],
                                           A[h % 2][:, s0:s0 + n], start=(j == 0), stop=(j == TT - 1),
                                           skip_group_check=True)
                ins.then_inc(pv_done, 1)

            def conv_average(src, done):
                for c in range(CT):
                    ins = nc.tensor.matmul(pA[1][:, :], avg[:, :], src[:, c, :], start=(c == 0), stop=(c == CT - 1))
                ins.then_inc(done, 1)

            for b in range(2):
                pe.wait_ge(tile_read[b], (J_MQ) // 2)
            pe.wait_ge(v_read, TT)
            pe.wait_ge(consts_round, 4)
            scores(0)
            scores(1)
            for h in range(HEADS):
                sums(h)
                if h:
                    head_out(h - 1)
                if h == 1:
                    pe.wait_ge(tap_done, CT * CONV_K)
                    conv_average(cacc, cmean_done)
                if h == 3:
                    pe.wait_ge(csq_made, CT)
                    conv_average(csq, cvar_done)
                if h + 2 < HEADS:
                    pe.wait_ge(a_made, 3 * (h + 1))
                    scores(h + 2)
            head_out(HEADS - 1)

            pe.wait_ge(a_made, 3 * HEADS)
            pe.wait_ge(clo_made, CT)
            pe.wait_ge(pv_lo, HEADS)
            for t in range(TT):
                tok_half(U_OUT, 0, t, mix_hi, mix_lo)
            for t in range(TT - 1):
                tok_half(U_OUT + RING, 1, t, mix_hi, mix_lo)
            turn2(G_LN1, 0, 0)
            tok_half(U_OUT + RING, 1, TT - 1, mix_hi, mix_lo)
            turn2(G_LN1, 1, 1)

            def mem_value(u):
                r = (u - U_MV) % RING
                for m in range(MT):
                    ins = tok_part(u, pA[m][:, :], mt_hi, mt_lo, m, 2 * r, r == 0, r == RING - 1)
                ins.then_inc(unit_used, 1)

            mem_value(U_MV)
            turn2(G_LN1, 2, 2)
            for r in range(1, RING):
                mem_value(U_MV + r)
            turn2(G_LN1, 3, 3)
            pe.wait_ge(mv_read, MT)
            for r in range(RING):
                mem_value(U_MV + RING + r)
            pe.wait_ge(tr_lo, G_LN2)
            pe.wait_ge(mv_read, 2 * MT)
            for i in range(KT):
                t_proj(U_MQ + i, J_MQ + i, xt_hi, xt_lo)

            def cross_scores(h):
                if h >= 2:
                    pe.wait_ge(cexp_made, TT * (h - 1))
                for t in range(TT):
                    for d in range(2):
                        k = 2 * h + d
                        ins = nc.tensor.matmul(pT[2 * (h % 2) + t // 2][:, MEM * (t % 2):MEM * (t % 2) + MEM],
                                               mqT[:, k, t * P:(t + 1) * P], mkT[:, k, :],
                                               start=(d == 0), stop=(d == 1))
                    if t % 2:
                        ins.then_inc(cs_done, 1)

            def cross_turn(h):
                pe.wait_ge(cp_made, TT * (h + 1))
                for m in range(MT):
                    for t in range(TT):
                        ins = nc.tensor.transpose(pX[m][:, t * P:(t + 1) * P], pr[h % 2][:, t, m * P:(m + 1) * P],
                                                  ident[:, :])
                    ins.then_inc(ct_done, 1)

            def cross_out(h):
                pe.wait_ge(ct_read0, h + 1)
                pe.wait_ge(ct_read1, h + 1)
                for d in range(2):
                    if h:
                        pe.wait_ge(co_lo, 2 * (h - 1) + d + 1)
                    c0 = h * MHD + d * P
                    for m in range(MT):
                        ins = nc.tensor.matmul(pA[d][:, :], mvtok[:, m, c0:c0 + P], prT[h % 2][:, m, :],
                                               start=(m == 0), stop=(m == MT - 1))
                    ins.then_inc(co_done, 1)

            for b in range(2):
                pe.wait_ge(tile_read[b], (J_MQ + KT) // 2)
            cross_scores(0)
            for h in range(MHEADS):
                if h + 1 < MHEADS:
                    cross_scores(h + 1)
                cross_turn(h)
                cross_out(h)

            pe.wait_ge(co_lo, 2 * MHEADS)
            for t in range(TT):
                tok_half(U_MO, 2, t, mix_hi, mix_lo)
            for t in range(TT - 1):
                tok_half(U_MO + RING, 3, t, mix_hi, mix_lo)
            turn2(G_LN2, 0, TT)
            tok_half(U_MO + RING, 3, TT - 1, mix_hi, mix_lo)
            for t in range(1, TT):
                turn2(G_LN2, t, TT + t)

            pe.wait_ge(tr_lo, G_LN2 + 2 * TT)
            for i in range(FT):
                if i >= 2:
                    pe.wait_ge(tv2, i - 1)
                t_tile(U_UP + 2 * i, bank[2 * (i % 2)][:, :], xt_hi, xt_lo).then_inc(unit_used, 1)
                if i >= 2:
                    pe.wait_ge(tg2, i - 1)
                t_tile(U_UP + 2 * i + 1, bank[2 * (i % 2) + 1][:, :], xt_hi, xt_lo).then_inc(unit_used, 1)

            for hf in range(2):
                for r0 in range(0, DN_HALF, RING):
                    n = min(RING, DN_HALF - r0)
                    if hf == 0:
                        pe.wait_ge(glo_made, 2 * (r0 + n))
                    for t in range(TT):
                        if hf and r0 == 0:
                            pe.wait_ge(tok_read, 4 * TT + t + 1)
                        tok_tile(U_DN + hf * DN_HALF + r0, n, t, tok_bank(2, t)[:, :], g_hi, g_lo, 2 * r0,
                                 r0 == 0, r0 + n == DN_HALF, tok_done)


_INS = ['x', 'mem', 'w_in', 'conv_w', 'conv_b', 'conv_ln_g', 'conv_ln_b', 'w_out', 'ln1_g', 'ln1_b',
        'mem_wq', 'mem_wk', 'mem_wv', 'mem_wo', 'ln2_g', 'ln2_b',
        'ffn_up', 'ffn_conv_w', 'ffn_conv_b', 'ffn_down', 'ln3_g', 'ln3_b']


def kernel(**inputs):
    import numpy as _np
    import concourse.bacc as _bacc
    from concourse import mybir as _mybir
    from concourse.bass_utils import run_bass_kernel_spmd as _run

    nc = _bacc.Bacc("TRN2", target_bir_lowering=False, num_devices=1)
    arrays, args = {}, []
    for name in _INS:
        a = _np.ascontiguousarray(inputs[name])
        arrays[f"in_{name}_dram"] = a
        args.append(nc.dram_tensor(f"in_{name}_dram", a.shape, _mybir.dt.from_np(a.dtype), kind="ExternalInput").ap())
    shape = inputs["x"].shape
    args.append(nc.dram_tensor("out_dram", shape, _mybir.dt.float32, kind="ExternalOutput").ap())
    decoder_layer(nc, *args)
    r = _run(nc, [arrays], core_ids=[0])
    return r.results[0]["out_dram"]
```

```python
from contextlib import ExitStack

import concourse.bass as bass
from concourse import mybir

F32 = mybir.dt.float32
F32R = mybir.dt.float32r
U8 = mybir.dt.uint8
ALU = mybir.AluOpType
ACT = mybir.ActivationFunctionType
AX = mybir.AxisListType

P = 128
CLAMP = 40.0
NEG = -1.0e30


def decoder_layer(nc, x, mem, w_in, conv_w, conv_b, conv_ln_g, conv_ln_b, w_out, ln1_g, ln1_b,
                  mem_wq, mem_wk, mem_wv, mem_wo, ln2_g, ln2_b,
                  ffn_up, ffn_conv_w, ffn_conv_b, ffn_down, ln3_g, ln3_b, out):
    _, SEQ, D = x.shape
    MEM = mem.shape[1]
    CONV_K, CH = conv_w.shape[1], conv_w.shape[2]
    FK, FF2 = ffn_conv_w.shape[1], ffn_conv_w.shape[2]
    FF = FF2 // 2
    HEADS, HD = 8, (D - CH) // 8
    MHEADS = 4
    MHD = D // MHEADS
    ALPHA = 2.0 ** 0.25
    EPS = 1e-5
    KT = D // P
    TT = SEQ // P
    MT = MEM // P
    CT = CH // P
    FT = FF // P
    H = D // 2
    QOFF, KOFF, VOFF = 2 * CH, 2 * CH + HEADS * HD, 2 * CH + 2 * HEADS * HD
    PAD = CONV_K - 1
    UP = SEQ + PAD

    RING = 4
    AHEAD = RING - 1
    UW = KT * P

    def t_unit(w, c0):
        return w[0, :, c0:c0 + P].rearrange("(k p) n -> p k n", p=P), "t"

    def tok_unit(w, r, c0):
        return w[0, r * 2 * P:(r + 1) * 2 * P, c0:c0 + H].rearrange("(k p) n -> p k n", p=P), "tok"

    units = []
    for c in range(CT):
        units += [t_unit(w_in, CH + c * P), t_unit(w_in, c * P)]
    U_QK = len(units)
    units += [t_unit(w_in, QOFF + i * P) for i in range(2 * HEADS * HD // P)]
    U_V = len(units)
    units += [tok_unit(w_in, r, VOFF) for r in range(KT // 2)]
    U_MK = len(units)
    units += [t_unit(mem_wk, i * P) for i in range(KT)]
    U_MV0 = len(units)
    units += [tok_unit(mem_wv, r, 0) for r in range(KT // 2)]
    U_OUT = len(units)
    units += [tok_unit(w_out, r, hf * H) for hf in range(2) for r in range(KT // 2)]
    U_MV1 = len(units)
    units += [tok_unit(mem_wv, r, H) for r in range(KT // 2)]
    U_MQ = len(units)
    units += [t_unit(mem_wq, i * P) for i in range(KT)]
    U_MO = len(units)
    units += [tok_unit(mem_wo, r, hf * H) for hf in range(2) for r in range(KT // 2)]
    U_UP = len(units)
    for i in range(FT):
        units += [t_unit(ffn_up, i * P), t_unit(ffn_up, FF + i * P)]
    U_DN = len(units)
    units += [tok_unit(ffn_down, r, hf * H) for hf in range(2) for r in range(FT // 2)]
    NU = len(units)
    DN_HALF = FT // 2

    with ExitStack() as ctx:
        def sem(name):
            return ctx.enter_context(nc.semaphore(name))

        SLAB = 207 * 1024
        SB0 = nc.lookup_mloc(ctx.enter_context(nc.sbuf_tensor("slab", [P, SLAB], U8))).addr
        at_ = [0]

        def place(name, shape, dt=F32, at=None):
            n = 4
            for s in shape[1:]:
                n *= s
            if at is None:
                at = at_[0]
                at_[0] += (n + 63) // 64 * 64
            assert at + n <= SLAB, (name, at, n)
            return nc.alloc_sbuf_tensor_at(name, shape, dt, offset=SB0 + at)

        w_raw = [place(f"w_raw{s}", [P, UW]) for s in range(RING)]
        w_hi = [place(f"w_hi{s}", [P, UW], F32R) for s in range(RING)]
        w_lo = [place(f"w_lo{s}", [P, UW], F32R) for s in range(RING)]
        xres = place("xres", [P, TT, D])
        xt_at = at_[0]
        xt_hi = place("xt_hi", [P, KT, SEQ], F32R)
        xt_lo = place("xt_lo", [P, KT, SEQ], F32R)
        ident = place("ident", [P, P])
        avg = place("avg", [P, P])
        ident_r = place("ident_r", [P, P], F32R)
        negtri_r = place("negtri_r", [P, P], F32R)
        negone_r = place("negone_r", [P, P], F32R)
        hide_r = place("hide_r", [P, P], F32R)
        cw = place("cw", [P, CT, CONV_K])
        cp = place("cp", [P, 3 * CT])
        fp = place("fp", [P, FK + 1, 2 * FT])
        lp = place("lp", [P, 4, KT])
        stats = place("stats", [P, TT, 12])
        mv = place("mv", [P, TT, 2])
        vareps = place("vareps", [P, TT])
        lnvar = place("lnvar", [P, TT])
        rstd = place("rstd", [P, TT])
        cmx = place("cmx", [P, MHEADS, TT])
        csum = place("csum", [P, MHEADS, TT])
        crec = place("crec", [P, MHEADS, TT])
        ln_gb = place("ln_gb", [P, 2, D])
        codd = nc.alloc_sbuf_tensor_at("codd", [P, SEQ], F32, offset=SB0 + at_[0] - 4 * 2 * D)
        reg = at_[0]
        KB = 1024
        qT = place("qT", [P, HEADS // 2, SEQ], at=reg)
        kT = place("kT", [P, HEADS // 2, SEQ], at=reg + 8 * KB)
        vtok = place("vtok", [P, TT, HEADS * HD], at=reg + 16 * KB)
        mix_hi = place("mix_hi", [P, KT, SEQ], F32R, at=reg + 24 * KB)
        mix_lo = place("mix_lo", [P, KT, SEQ], F32R, at=reg + 40 * KB)
        mt_hi = place("mt_hi", [P, KT, MEM], F32R, at=reg + 56 * KB)
        mt_lo = place("mt_lo", [P, KT, MEM], F32R, at=reg + 64 * KB)
        mkT = place("mkT", [P, KT, MEM], at=reg + 72 * KB)
        memtok = place("memtok", [P, MT, D], at=reg + 72 * KB)
        cacc = place("cacc", [P, CT, SEQ], at=reg + 80 * KB)
        upad = place("upad", [P, CT, UP], at=reg + 88 * KB)
        csq = place("csq", [P, CT, SEQ], at=reg + 88 * KB)
        cw_rows = place("cw_rows", [CONV_K, CH], at=reg + 24 * KB)
        cp_rows = place("cp_rows", [3 * CT, P], at=reg + 27 * KB)
        fp_rows = place("fp_rows", [2 * FT, FK + 1, P], at=reg + 28 * KB)
        lp_rows = place("lp_rows", [4 * KT, P], at=reg + 31 * KB)
        negtri = place("negtri", [P, P], at=reg + 44 * KB)
        negone = place("negone", [P, P], at=reg + 45 * KB)
        hide = place("hide", [P, P], at=reg + 46 * KB)
        sig = place("sig", [P, SEQ], at=reg + 40 * KB)
        crstd = place("crstd", [P, SEQ], at=reg + 40 * KB)
        SW = 1280
        E = [place(f"E{i}", [P, SW], at=xt_at + 5 * KB * i) for i in range(2)]
        sp_lo = [place(f"sp_lo{i}", [P, SW], F32R, at=xt_at + 5 * KB * i) for i in range(2)]
        sp_hi = [place(f"sp_hi{i}", [P, SW], F32R, at=xt_at + 5 * KB * (2 + i)) for i in range(2)]
        A = [place(f"A{i}", [P, SW], at=xt_at + 5 * KB * (4 + i)) for i in range(2)]
        xaff = [place(f"xaff{i}", [P, 4, P], at=reg + (80 + 2 * i) * KB) for i in range(2)]
        mvtok = place("mvtok", [P, MT, D], at=reg)
        mqT = place("mqT", [P, KT, SEQ], at=reg + 8 * KB)
        pr = [place(f"pr{i}", [P, TT, MEM], at=reg + (56 + 4 * i) * KB) for i in range(2)]
        prT = [place(f"prT{i}", [P, MT, SEQ], at=reg + (64 + 4 * i) * KB) for i in range(2)]
        g_hi = place("g_hi", [P, FT, SEQ], F32R, at=reg)
        g_lo = place("g_lo", [P, FT, SEQ], F32R, at=reg + 4 * FT * SEQ)
        f0 = reg + 8 * FT * SEQ
        yv = [place(f"yv{i}", [P, SEQ], at=f0 + 2 * KB * i) for i in range(2)]
        yg = [place(f"yg{i}", [P, SEQ], at=f0 + 2 * KB * (2 + i)) for i in range(2)]

        bank = [ctx.enter_context(nc.psum_tensor(f"bank{i}", [P, SEQ], F32)) for i in range(8)]
        pA = bank[0:2]
        pT = bank[2:6]
        pX = bank[6:8]

        x_loaded = [sem(f"x_loaded{t}") for t in range(TT)]
        mem_loaded = sem("mem_loaded")
        rows_loaded = sem("rows_loaded")
        ln_loaded = sem("ln_loaded")
        raw_loaded = [sem(f"raw_loaded{s}") for s in range(RING)]
        hi_made, lo_made, unit_used = sem("hi_made"), sem("lo_made"), sem("unit_used")
        consts_made, consts_round = sem("consts_made"), sem("consts_round")
        pad_zeroed = sem("pad_zeroed")
        tr_done, tr_hi, tr_lo = sem("tr_done"), sem("tr_hi"), sem("tr_lo")
        rows_turned, params_ready = sem("rows_turned"), sem("params_ready")
        tile_read = [sem("tile_read0"), sem("tile_read1")]
        sig_made, u_made = sem("sig_made"), sem("u_made")
        tap_done = sem("tap_done")
        v_done, v_read = sem("v_done"), sem("v_read")
        z_done, clamp_made, exp_made, ln_made = sem("z_done"), sem("clamp_made"), sem("exp_made"), sem("ln_made")
        sp_made, sphi_made, splo_made = sem("sp_made"), sem("sphi_made"), sem("splo_made")
        s_done, a_made = sem("s_done"), sem("a_made")
        pv_done, pv_hi, pv_lo = sem("pv_done"), sem("pv_hi"), sem("pv_lo")
        cmean_done, ccent_made, csq_made = sem("cmean_done"), sem("ccent_made"), sem("csq_made")
        cvar_done, cln_made, crstd_made = sem("cvar_done"), sem("cln_made"), sem("crstd_made")
        cnorm_made, cact_made, chi_made, clo_made = sem("cnorm_made"), sem("cact_made"), sem("chi_made"), sem("clo_made")
        cve_made = sem("cve_made")
        tok_done, tok_read = sem("tok_done"), sem("tok_read")
        st_made, ag_made, ve_made, lv_made, rs_made = sem("st_made"), sem("ag_made"), sem("ve_made"), sem("lv_made"), sem("rs_made")
        gain_made, ln_made2 = sem("gain_made"), sem("ln_done")
        norm_made, aff_made, aff1_made = sem("norm_made"), sem("aff_made"), sem("aff1_made")
        mv_read = sem("mv_read")
        cs_done, cmax_made, cexp_made = sem("cs_done"), sem("cmax_made"), sem("cexp_made")
        crec_made, cp_made = sem("crec_made"), sem("cprob_made")
        ct_done, ct_read0, ct_read1 = sem("ct_done"), sem("ct_read0"), sem("ct_read1")
        co_done, co_hi, co_lo = sem("co_done"), sem("co_hi"), sem("co_lo")
        yv_made, yg_made = sem("yv_made"), sem("yg_made")
        tv1, tg1, tv2, tg2 = sem("tapv1"), sem("tapg1"), sem("tapv2"), sem("tapg2")
        silu_made, gm_made, ghi_made, glo_made = sem("silu_made"), sem("gm_made"), sem("ghi_made"), sem("glo_made")
        stored = sem("stored")

        LATE = 2
        J_QK, J_MK, J_MQ = 0, 2 * TT, 2 * TT + KT
        TILE_BANK = [0, 1] * TT + [0, 1] * ((KT - LATE) // 2) + [1] * LATE + [0, 1] * (KT // 2)

        H_MEAN, H_SQUARE, H_VAR, H_RSTD, H_SILU, H_PARTS = 2, 3, 4, 5, 6, 7

        def tiles_before(j, b):
            return TILE_BANK[:j].count(b)

        G_MEM, G_LN1, G_LN2 = 2 * TT, 2 * TT + 2 * MT, 4 * TT + 2 * MT

        def turn_bank(g):
            if G_MEM <= g < G_LN1:
                return pT[g - G_MEM]
            if g < G_LN1:
                return (pX + pT)[g % 6]
            return (pX[0], pX[1], pT[0], pT[1], pX[0], pX[1], pT[2], pT[3])[(g - G_LN1) % (2 * TT)]

        SEG = {0: (0, 0, 0), 1: (1, 0, 512), 3: (1, 384, 896), 2: (2, 0, 1024)}
        BANKW = [(0, 512), (512, 512), (1024, 256)]

        def zbank(h, b):
            return (pT[0], pT[1], pX[0])[b] if h % 2 == 0 else (pT[2], pT[3], pX[1])[b]

        HALF_END = [U_OUT + RING, U_OUT + 2 * RING, U_MO + RING, U_MO + 2 * RING, U_DN + DN_HALF, U_DN + 2 * DN_HALF]

        def tok_bank(layer, t):
            return bank[4 + t] if layer == 2 else pT[t]

        block = ctx.enter_context(nc.Block())

        @block.sync
        def _(sp):
            def load_unit(u):
                s = u % RING
                if u >= RING:
                    sp.wait_ge(lo_made, u - RING + 1)
                src, _ = units[u]
                k = src.shape[1]
                sp.dma_start(w_raw[s][:, :].rearrange("p (k n) -> p k n", k=k), src).then_inc(raw_loaded[s], 16)

            def load_ln(g, b):
                for i, v in enumerate((g, b)):
                    sp.dma_start(ln_gb[:, i, :], v[0:1, :].broadcast_to([P, D])).then_inc(ln_loaded, 16)

            for t in range(TT):
                if t == TT - 1:
                    load_unit(0)
                sp.dma_start(xres[:, t, :], x[0, t * P:(t + 1) * P, :]).then_inc(x_loaded[t], 16)
            for u in range(1, NU):
                load_unit(u)
                if u == 1:
                    sp.dma_start(cw_rows[:, :], conv_w[0]).then_inc(rows_loaded, 16)
                    for i, v in enumerate((conv_b, conv_ln_g, conv_ln_b)):
                        sp.dma_start(cp_rows[i * CT:(i + 1) * CT, :],
                                     v[0].rearrange("(c p) -> c p", p=P)).then_inc(rows_loaded, 16)
                    sp.dma_start(fp_rows[:, 0:FK, :], ffn_conv_w[0].rearrange("k (c p) -> c k p", p=P)).then_inc(rows_loaded, 16)
                    for i, v in enumerate((ln1_g, ln1_b, ln2_g, ln2_b)):
                        sp.dma_start(lp_rows[i * KT:(i + 1) * KT, :],
                                     v[0].rearrange("(c p) -> c p", p=P)).then_inc(rows_loaded, 16)
                    sp.dma_start(fp_rows[:, FK, :], ffn_conv_b[0].rearrange("(c p) -> c p", p=P)).then_inc(rows_loaded, 16)
                if u == RING - 1:
                    sp.dma_start(memtok[:, :, :], mem[0].rearrange("(t p) d -> p t d", p=P)).then_inc(mem_loaded, 16)
                if u == U_OUT:
                    sp.wait_ge(tap_done, CT * (CONV_K + 1))
                    load_ln(ln1_g, ln1_b)
                if u == U_MO + AHEAD:
                    sp.wait_ge(ln_made2, TT)
                    load_ln(ln2_g, ln2_b)
                if u == U_DN:
                    sp.wait_ge(ln_made2, 2 * TT)
                    load_ln(ln3_g, ln3_b)
            for t in range(TT):
                sp.wait_ge(ln_made2, 2 * TT + t + 1)
                sp.dma_start(out[0, t * P:(t + 1) * P, :], xres[:, t, :]).then_inc(stored, 16)
            sp.wait_ge(stored, 16 * TT)

        @block.gpsimd
        def _(pool):
            nc.gpsimd.memset(ident[:, :], 0.0).then_inc(consts_made, 1)
            nc.gpsimd.memset(negtri[:, :], -1.0).then_inc(consts_made, 1)
            nc.gpsimd.memset(negone[:, :], -1.0).then_inc(consts_made, 1)
            nc.gpsimd.memset(hide[:, :], 0.0).then_inc(consts_made, 1)
            nc.gpsimd.memset(avg[:, :], 1.0 / CH).then_inc(consts_made, 1)
            pool.wait_ge(consts_made, 5)
            nc.gpsimd.affine_select(out=ident[:, :], in_=ident[:, :], compare_op=ALU.not_equal, fill=1.0, base=0,
                                    pattern=[[-1, P]], channel_multiplier=1).then_inc(consts_made, 1)
            nc.gpsimd.affine_select(out=negtri[:, :], in_=negtri[:, :], compare_op=ALU.is_ge, fill=0.0, base=0,
                                    pattern=[[-1, P]], channel_multiplier=1).then_inc(consts_made, 1)
            nc.gpsimd.affine_select(out=hide[:, :], in_=hide[:, :], compare_op=ALU.is_gt, fill=NEG, base=0,
                                    pattern=[[1, P]], channel_multiplier=-1).then_inc(consts_made, 1)
            nc.gpsimd.memset(upad[:, :, 0:PAD], 0.0).then_inc(pad_zeroed, 1)

        @block.scalar
        def _(act):
            def convert(u):
                if u >= NU:
                    return
                s = u % RING
                act.wait_ge(raw_loaded[s], 16 * (u // RING + 1))
                if u >= RING:
                    act.wait_ge(unit_used, u - RING + 1)
                nc.scalar.copy(w_hi[s][:, :], w_raw[s][:, :]).then_inc(hi_made, 1)

            def turn_hi(g, dst, t):
                act.wait_ge(tr_done, g + 1)
                nc.scalar.copy(dst[:, 4 * (g % 2):4 * (g % 2) + 4, t * P:(t + 1) * P],
                               turn_bank(g)[:, :].rearrange("p (k n) -> p k n", k=4)).then_inc(tr_hi, 1)

            def tile(u, j, dst, scale=1.0):
                act.wait_ge(unit_used, u + 1)
                n = dst.shape[1]
                b = TILE_BANK[j]
                nc.scalar.activation(dst, pA[b][:, 0:n], ACT.Copy, scale=scale).then_inc(tile_read[b], 1)

            nc.scalar.preload_act_table_set("sigmoid_and_others")
            for t in range(TT):
                if t == TT - 1:
                    convert(0)
                for hf in range(2):
                    turn_hi(2 * t + hf, xt_hi, t)
            for u in range(1, AHEAD):
                convert(u)
            for c in range(CT):
                convert(2 * c + AHEAD)
                act.wait_ge(unit_used, 2 * c + 1)
                if c:
                    act.wait_ge(u_made, c)
                nc.scalar.activation(sig[:, :], pA[0][:, :], ACT.Sigmoid).then_inc(sig_made, 1)
                if c == 0:
                    act.wait_ge(rows_turned, 1)
                    nc.scalar.copy(cw[:, :, :], pT[0][:, 0:CT * CONV_K].rearrange("p (c k) -> p c k", c=CT)).then_inc(params_ready, 1)
                    nc.scalar.copy(cp[:, :], pT[1][:, 0:3 * CT]).then_inc(params_ready, 1)
                    nc.scalar.copy(lp[:, :, :], pT[1][:, P:P + 4 * KT].rearrange("p (i k) -> p i k", i=4)).then_inc(params_ready, 1)
                    nc.scalar.copy(fp[:, :, :], pT[2][:, 0:(FK + 1) * 2 * FT].rearrange("p (k c) -> p k c", k=FK + 1)).then_inc(params_ready, 1)
                convert(2 * c + 1 + AHEAD)
            for t in range(MT):
                for hf in range(2):
                    turn_hi(G_MEM + 2 * t + hf, mt_hi, t)
            act.wait_ge(consts_made, 8)
            for dst, src in ((ident_r, ident), (negtri_r, negtri), (negone_r, negone), (hide_r, hide)):
                nc.scalar.copy(dst[:, :], src[:, :]).then_inc(consts_round, 1)
            for i in range(8):
                convert(U_QK + i + AHEAD)
                dst = (qT if i < 4 else kT)[:, i % 4, :]
                tile(U_QK + i, J_QK + i, dst, HD ** -0.5 if i < 4 else 1.0)
            convert(U_V + AHEAD)
            for t in range(TT):
                if t == TT - 1:
                    for u in range(3):
                        convert(U_V + RING + u)
                if t < TT - 1:
                    act.wait_ge(v_done, t + 1)
                else:
                    act.wait_ge(unit_used, U_V + RING)
                nc.scalar.copy(vtok[:, t, :], pT[t][:, :]).then_inc(v_read, 1)
            def softplus_parts(h):
                for b, (c0, w) in enumerate(BANKW):
                    act.wait_ge(clamp_made, 3 * h + b + 1)
                    e = E[h % 2][:, c0:c0 + w]
                    nc.scalar.activation(e, e, ACT.Exp).then_inc(exp_made, 1)
                for b, (c0, w) in enumerate(BANKW):
                    act.wait_ge(exp_made, 3 * h + b + 1)
                    e = E[h % 2][:, c0:c0 + w]
                    nc.scalar.activation(e, e, ACT.Ln, bias=1.0).then_inc(ln_made, 1)

            def weights_of(h):
                for b, (c0, w) in enumerate(BANKW):
                    act.wait_ge(s_done, 3 * h + b + 1)
                    nc.scalar.activation(A[h % 2][:, c0:c0 + w], zbank(h, b)[:, 0:w], ACT.Exp).then_inc(a_made, 1)

            def head_out_hi(h):
                act.wait_ge(pv_done, h + 1)
                p0 = HD * (h % 2)
                nc.scalar.copy(mix_hi[p0:p0 + HD, CT + h // 2, :], pA[0][p0:p0 + HD, :]).then_inc(pv_hi, 1)

            nc.scalar.preload_act_table_set("natural_log_exp_and_others")
            for i in range(KT - LATE):
                convert(U_MK + i + AHEAD)
                tile(U_MK + i, J_MK + i, mkT[:, i, :])
                if i == 2:
                    softplus_parts(0)
                if i == 5:
                    softplus_parts(1)
            for h in range(HEADS):
                if h <= LATE:
                    convert(U_MV0 - LATE + h + AHEAD)
                weights_of(h)
                if h < LATE:
                    i = KT - LATE + h
                    tile(U_MK + i, J_MK + i, mkT[:, i, :])
                if h:
                    head_out_hi(h - 1)
                if h == H_SQUARE:
                    for c in range(CT):
                        act.wait_ge(ccent_made, c + 1)
                        nc.scalar.activation(csq[:, c, :], cacc[:, c, :], ACT.Square).then_inc(csq_made, 1)
                if h == H_RSTD:
                    act.wait_ge(cve_made, 1)
                    nc.scalar.activation(crstd[:, :], crstd[:, :], ACT.Ln).then_inc(cln_made, 1)
                    act.wait_ge(cln_made, 1)
                    nc.scalar.activation(crstd[:, :], crstd[:, :], ACT.Exp, scale=-0.5).then_inc(crstd_made, 1)
                if h + 2 < HEADS:
                    softplus_parts(h + 2)
                if h == H_SILU:
                    for c in range(CT):
                        act.wait_ge(cnorm_made, c + 1)
                        nc.scalar.activation(cacc[:, c, :], cacc[:, c, :], ACT.Silu, scale=cp[:, CT + c:CT + c + 1],
                                             bias=cp[:, 2 * CT + c:2 * CT + c + 1]).then_inc(cact_made, 1)
                    nc.scalar.preload_act_table_set("natural_log_exp_and_others")
            convert(U_MV0 + RING)
            convert(U_MV0 + RING + 1)
            head_out_hi(HEADS - 1)
            convert(U_MV0 + RING + 2)
            convert(U_MV0 + RING + 3)

            def mem_values(hf, banks):
                act.wait_ge(unit_used, (U_MV0, U_MV1)[hf] + RING)
                for m in range(MT):
                    nc.scalar.copy(mvtok[:, m, hf * H:(hf + 1) * H], banks[m][:, :]).then_inc(mv_read, 1)

            mem_values(0, (pA[1], pX[0]))

            def ln_rstd(n):
                t = n % TT
                act.wait_ge(ve_made, n + 1)
                nc.scalar.activation(lnvar[:, t:t + 1], vareps[:, t:t + 1], ACT.Ln).then_inc(lv_made, 1)
                act.wait_ge(lv_made, n + 1)
                nc.scalar.activation(rstd[:, t:t + 1], lnvar[:, t:t + 1], ACT.Exp, scale=-0.5).then_inc(rs_made, 1)

            def turn2(g0, t):
                layer = 0 if g0 == G_LN1 else 1
                n = layer * TT + t
                g = g0 + 2 * t
                act.wait_ge(tr_done, g + 1)
                if n:
                    act.wait_ge(tr_lo, G_LN1 + 2 * n - 1)
                for k in range(4):
                    ins = nc.scalar.activation(xaff[0][:, k, :], turn_bank(g)[:, k * P:(k + 1) * P], ACT.Identity,
                                               scale=lp[:, 2 * layer, k:k + 1], bias=lp[:, 2 * layer + 1, k:k + 1])
                ins.then_inc(aff_made, 1)
                act.wait_ge(aff_made, n + 1)
                nc.scalar.copy(xt_hi[:, 0:4, t * P:(t + 1) * P], xaff[0][:, :, :]).then_inc(tr_hi, 1)
                act.wait_ge(aff1_made, n + 1)
                nc.scalar.copy(xt_hi[:, 4:8, t * P:(t + 1) * P], xaff[1][:, :, :]).then_inc(tr_hi, 1)

            for u in range(4):
                convert(U_OUT + RING + u)
            ln_rstd(0)
            ln_rstd(1)
            turn2(G_LN1, 0)
            ln_rstd(2)
            turn2(G_LN1, 1)
            convert(U_MV1)
            convert(U_MV1 + 1)
            ln_rstd(3)
            convert(U_MV1 + 2)
            turn2(G_LN1, 2)
            convert(U_MV1 + 3)
            convert(U_MQ)
            turn2(G_LN1, 3)
            convert(U_MQ + 1)
            convert(U_MQ + 2)
            mem_values(1, pT)
            def cross_exp(h):
                act.wait_ge(cmax_made, h + 1)
                if h >= 2:
                    act.wait_ge(ct_done, MT * (h - 1))
                for t in range(TT):
                    nc.scalar.activation(pr[h % 2][:, t, :], pT[2 * (h % 2) + t // 2][:, MEM * (t % 2):MEM * (t % 2) + MEM],
                                         ACT.Exp, bias=cmx[:, h, t:t + 1],
                                         accum_out=csum[:, h, t:t + 1]).then_inc(cexp_made, 1)

            def cross_turn0(h):
                act.wait_ge(ct_done, MT * h + 1)
                if h >= 2:
                    act.wait_ge(co_done, 2 * (h - 1))
                nc.scalar.copy(prT[h % 2][:, 0, :], pX[0][:, :]).then_inc(ct_read0, 1)

            def cross_out_hi(h):
                for d in range(2):
                    act.wait_ge(co_done, 2 * h + d + 1)
                    nc.scalar.copy(mix_hi[:, 2 * h + d, :], pA[d][:, :]).then_inc(co_hi, 1)

            for i in range(KT):
                convert(U_MQ + i + AHEAD)
                tile(U_MQ + i, J_MQ + i, mqT[:, i, :], MHD ** -0.5)
                if i == 5:
                    cross_exp(0)
                if i == 7:
                    cross_exp(1)

            cross_turn0(0)
            for h in range(MHEADS):
                if h + 2 < MHEADS:
                    cross_exp(h + 2)
                if h + 1 < MHEADS:
                    cross_turn0(h + 1)
                cross_out_hi(h)

            convert(U_MO + AHEAD)
            for u in range(4):
                convert(U_MO + RING + u)
            ln_rstd(TT + 0)
            ln_rstd(TT + 1)
            turn2(G_LN2, 0)
            ln_rstd(TT + 2)
            turn2(G_LN2, 1)
            convert(U_UP)
            convert(U_UP + 1)
            ln_rstd(TT + 3)
            turn2(G_LN2, 2)
            convert(U_UP + 2)
            turn2(G_LN2, 3)

            def ffn_silu(i):
                act.wait_ge(tg2, i + 1)
                nc.scalar.activation(yg[i % 2][:, :], yg[i % 2][:, :], ACT.Silu).then_inc(silu_made, 1)

            for i in range(FT):
                convert(U_UP + 2 * i + AHEAD)
                if i >= 2:
                    act.wait_ge(glo_made, i - 1)
                act.wait_ge(unit_used, U_UP + 2 * i + 1)
                nc.scalar.activation(yv[i % 2][:, :], bank[2 * (i % 2)][:, :], ACT.Identity,
                                     scale=fp[:, FK - 1, i:i + 1], bias=fp[:, FK, i:i + 1]).then_inc(yv_made, 1)
                convert(U_UP + 2 * i + 1 + AHEAD)
                act.wait_ge(unit_used, U_UP + 2 * i + 2)
                nc.scalar.activation(yg[i % 2][:, :], bank[2 * (i % 2) + 1][:, :], ACT.Identity,
                                     scale=fp[:, FK - 1, FT + i:FT + i + 1], bias=fp[:, FK, FT + i:FT + i + 1]).then_inc(yg_made, 1)
                if i == FT - 1:
                    convert(U_DN + AHEAD)
                if i:
                    ffn_silu(i - 1)
            ffn_silu(FT - 1)
            nc.scalar.preload_act_table_set("natural_log_exp_and_others")
            for u in range(U_DN + RING, NU):
                convert(u)
            for t in range(TT):
                ln_rstd(2 * TT + t)

        @block.vector
        def _(dve):
            def convert(u):
                if u >= NU:
                    return
                s = u % RING
                dve.wait_ge(hi_made, u + 1)
                nc.vector.tensor_tensor(w_lo[s][:, :], w_raw[s][:, :], w_hi[s][:, :].bitcast(F32),
                                        ALU.subtract).then_inc(lo_made, 1)

            def turn_lo(g, hi, lo, t):
                dve.wait_ge(tr_hi, g + 1)
                k0 = 4 * (g % 2)
                nc.vector.tensor_tensor(lo[:, k0:k0 + 4, t * P:(t + 1) * P],
                                        turn_bank(g)[:, :].rearrange("p (k n) -> p k n", k=4),
                                        hi[:, k0:k0 + 4, t * P:(t + 1) * P].bitcast(F32), ALU.subtract).then_inc(tr_lo, 1)

            taps = [(c, j) for c in range(CT) for j in range(CONV_K + 1)]
            at = [0]

            def conv_taps(n):
                for c, j in taps[at[0]:at[0] + n]:
                    y = (cacc[:, c, :], codd[:, :])[j % 2]
                    if j == 0:
                        dve.wait_ge(u_made, c + 1)
                    if at[0] >= 2:
                        dve.wait_ge(tap_done, at[0] - 1 if j < CONV_K else at[0])
                    if j == CONV_K:
                        ins = nc.vector.tensor_tensor(cacc[:, c, :], cacc[:, c, :], codd[:, :], ALU.add)
                    elif j < 2:
                        ins = nc.vector.tensor_scalar(y, upad[:, c, j:j + SEQ], cw[:, c, j:j + 1],
                                                      (cp[:, c:c + 1], 0.0)[j], ALU.mult, ALU.add)
                    else:
                        ins = nc.vector.scalar_tensor_tensor(y, upad[:, c, j:j + SEQ], cw[:, c, j:j + 1], y,
                                                             ALU.mult, ALU.add)
                    ins.then_inc(tap_done, 1)
                    at[0] += 1

            for t in range(TT):
                if t == TT - 1:
                    convert(0)
                for hf in range(2):
                    turn_lo(2 * t + hf, xt_hi, xt_lo, t)
            for u in range(1, AHEAD):
                convert(u)
            dve.wait_ge(pad_zeroed, 1)
            for c in range(CT):
                convert(2 * c + AHEAD)
                if c:
                    conv_taps(6)
                convert(2 * c + 1 + AHEAD)
                dve.wait_ge(unit_used, 2 * c + 2)
                dve.wait_ge(sig_made, c + 1)
                nc.vector.tensor_tensor(upad[:, c, PAD:UP], pA[1][:, :], sig[:, :], ALU.mult).then_inc(u_made, 1)
                if c == 0:
                    dve.wait_ge(params_ready, 4)
                conv_taps(6)
            for t in range(MT):
                for hf in range(2):
                    turn_lo(G_MEM + 2 * t + hf, mt_hi, mt_lo, t)
            for i in range(8):
                convert(U_QK + i + AHEAD)
                conv_taps(5)
            convert(U_V + AHEAD)
            conv_taps(26)
            for u in range(3):
                convert(U_V + RING + u)

            def scores_clamp(h):
                for b, (c0, w) in enumerate(BANKW):
                    dve.wait_ge(z_done, 3 * h + b + 1)
                    nc.vector.tensor_scalar(E[h % 2][:, c0:c0 + w], zbank(h, b)[:, 0:w], CLAMP, None,
                                            ALU.min).then_inc(clamp_made, 1)

            def softplus(h):
                for b, (c0, w) in enumerate(BANKW):
                    dve.wait_ge(ln_made, 3 * h + b + 1)
                    e = E[h % 2][:, c0:c0 + w]
                    nc.vector.tensor_tensor(e, zbank(h, b)[:, 0:w], e, ALU.max).then_inc(sp_made, 1)
                for b, (c0, w) in enumerate(BANKW):
                    dve.wait_ge(sp_made, 3 * h + b + 1)
                    nc.vector.tensor_copy(sp_hi[h % 2][:, c0:c0 + w], E[h % 2][:, c0:c0 + w]).then_inc(sphi_made, 1)
                for b, (c0, w) in enumerate(BANKW):
                    dve.wait_ge(sphi_made, 3 * h + b + 1)
                    nc.vector.tensor_tensor(sp_lo[h % 2][:, c0:c0 + w], E[h % 2][:, c0:c0 + w],
                                            sp_hi[h % 2][:, c0:c0 + w].bitcast(F32), ALU.subtract).then_inc(splo_made, 1)

            def head_out_lo(h):
                dve.wait_ge(pv_hi, h + 1)
                p0 = HD * (h % 2)
                nc.vector.tensor_tensor(mix_lo[p0:p0 + HD, CT + h // 2, :], pA[0][p0:p0 + HD, :],
                                        mix_hi[p0:p0 + HD, CT + h // 2, :].bitcast(F32), ALU.subtract).then_inc(pv_lo, 1)

            for i in range(KT - LATE):
                convert(U_MK + i + AHEAD)
                if i == 1:
                    scores_clamp(0)
                if i == 3:
                    softplus(0)
                if i == 4:
                    scores_clamp(1)
                conv_taps(4 if i < 3 else 1)
            softplus(1)
            conv_taps(3)
            for h in range(HEADS):
                if h <= LATE:
                    convert(U_MV0 - LATE + h + AHEAD)
                if h == H_MEAN:
                    conv_taps(len(taps))
                if h:
                    head_out_lo(h - 1)
                if h + 2 < HEADS:
                    scores_clamp(h + 2)
                if h == H_MEAN:
                    dve.wait_ge(cmean_done, 1)
                    for c in range(CT):
                        nc.vector.tensor_tensor(cacc[:, c, :], cacc[:, c, :], pA[1][:, :], ALU.subtract).then_inc(ccent_made, 1)
                if h == H_VAR:
                    dve.wait_ge(cvar_done, 1)
                    nc.vector.tensor_scalar(crstd[:, :], pA[1][:, :], EPS, None, ALU.add).then_inc(cve_made, 1)
                if h == H_RSTD:
                    dve.wait_ge(crstd_made, 1)
                    for c in range(CT):
                        nc.vector.tensor_tensor(cacc[:, c, :], cacc[:, c, :], crstd[:, :], ALU.mult).then_inc(cnorm_made, 1)
                if h == H_PARTS:
                    for c in range(CT):
                        dve.wait_ge(cact_made, c + 1)
                        nc.vector.tensor_copy(mix_hi[:, c, :], cacc[:, c, :]).then_inc(chi_made, 1)
                    for c in range(CT):
                        dve.wait_ge(chi_made, c + 1)
                        nc.vector.tensor_tensor(mix_lo[:, c, :], cacc[:, c, :], mix_hi[:, c, :].bitcast(F32),
                                                ALU.subtract).then_inc(clo_made, 1)
                if h + 2 < HEADS:
                    softplus(h + 2)
                if h < H_MEAN:
                    conv_taps(3)
            convert(U_MV0 + RING)
            convert(U_MV0 + RING + 1)
            head_out_lo(HEADS - 1)
            convert(U_MV0 + RING + 2)
            convert(U_MV0 + RING + 3)

            def residual(n, hf):
                t = n % TT
                half = 2 * (n // TT) + hf
                idx = half * TT + t
                if t < TT - 1:
                    dve.wait_ge(tok_done, (TT - 1) * half + t + 1)
                else:
                    dve.wait_ge(unit_used, HALF_END[half])
                if half and hf == 0:
                    dve.wait_ge(ln_made2, TT * (n // TT - 1) + t + 1)
                xs = xres[:, t, hf * H:(hf + 1) * H]
                nc.vector.scalar_tensor_tensor(xs, xs, ALPHA, tok_bank(n // TT, t)[:, :], ALU.mult, ALU.add).then_inc(tok_read, 1)
                dve.wait_ge(tok_read, idx + 1)
                nc.vector.bn_stats(stats[:, t, 6 * hf:6 * hf + 6], xs).then_inc(st_made, 1)
                return idx

            def moments(n):
                t = n % TT
                idx = residual(n, 1)
                dve.wait_ge(st_made, idx + 1)
                nc.vector.bn_aggr(mv[:, t, :], stats[:, t, :]).then_inc(ag_made, 1)
                dve.wait_ge(ag_made, n + 1)
                nc.vector.tensor_scalar(vareps[:, t:t + 1], mv[:, t, 1:2], EPS, None, ALU.add).then_inc(ve_made, 1)

            def normalize(n):
                moments(n)
                t = n % TT
                dve.wait_ge(rs_made, n + 1)
                nc.vector.tensor_scalar(xres[:, t, :], xres[:, t, :], mv[:, t, 0:1], rstd[:, t:t + 1],
                                        ALU.subtract, ALU.mult).then_inc(norm_made, 1)

            def gains(layer, t, i):
                n = layer * TT + t
                if i == 0:
                    dve.wait_ge(tr_done, (G_LN1, G_LN2)[layer] + 2 * t + 2)
                    dve.wait_ge(ln_loaded, 32 * (layer + 1))
                    nc.vector.tensor_tensor(xres[:, t, :], xres[:, t, :], ln_gb[:, 0, :], ALU.mult).then_inc(gain_made, 1)
                else:
                    dve.wait_ge(gain_made, n + 1)
                    nc.vector.tensor_tensor(xres[:, t, :], xres[:, t, :], ln_gb[:, 1, :], ALU.add).then_inc(ln_made2, 1)

            def last_norm(n):
                moments(n)
                t = n % TT
                if t == 0:
                    dve.wait_ge(ln_loaded, 32 * 3)
                nc.vector.scalar_tensor_tensor(xres[:, t, :], xres[:, t, :], mv[:, t, 0:1], ln_gb[:, 0, :],
                                               ALU.subtract, ALU.mult).then_inc(gain_made, 1)
                dve.wait_ge(gain_made, n + 1)
                dve.wait_ge(rs_made, n + 1)
                nc.vector.scalar_tensor_tensor(xres[:, t, :], xres[:, t, :], rstd[:, t:t + 1], ln_gb[:, 1, :],
                                               ALU.mult, ALU.add).then_inc(ln_made2, 1)

            def turn2(g0, t):
                layer = 0 if g0 == G_LN1 else 1
                g = g0 + 2 * t
                dve.wait_ge(tr_done, g + 2)
                if g > G_LN1:
                    dve.wait_ge(tr_lo, g)
                for k in range(4):
                    ins = nc.vector.tensor_scalar(xaff[1][:, k, :], turn_bank(g + 1)[:, k * P:(k + 1) * P],
                                                  lp[:, 2 * layer, 4 + k:5 + k], lp[:, 2 * layer + 1, 4 + k:5 + k],
                                                  ALU.mult, ALU.add)
                ins.then_inc(aff1_made, 1)
                for hf in range(2):
                    dve.wait_ge(tr_hi, g + hf + 1)
                    k0 = 4 * hf
                    nc.vector.tensor_tensor(xt_lo[:, k0:k0 + 4, t * P:(t + 1) * P], xaff[hf][:, :, :],
                                            xt_hi[:, k0:k0 + 4, t * P:(t + 1) * P].bitcast(F32),
                                            ALU.subtract).then_inc(tr_lo, 1)

            for t in range(TT - 1):
                residual(t, 0)
            for u in range(3):
                convert(U_OUT + RING + u)
            residual(TT - 1, 0)
            convert(U_OUT + RING + 3)
            normalize(0)
            normalize(1)
            turn2(G_LN1, 0)
            normalize(2)
            turn2(G_LN1, 1)
            convert(U_MV1)
            convert(U_MV1 + 1)
            normalize(3)
            convert(U_MV1 + 2)
            turn2(G_LN1, 2)
            convert(U_MV1 + 3)
            convert(U_MQ)
            turn2(G_LN1, 3)
            convert(U_MQ + 1)
            convert(U_MQ + 2)

            def cross_max(h):
                for i in range(2):
                    dve.wait_ge(cs_done, 2 * h + i + 1)
                    ins = nc.vector.tensor_reduce(cmx[:, h, 2 * i:2 * i + 2],
                                                  pT[2 * (h % 2) + i][:, :].rearrange("p (t m) -> p t m", t=2),
                                                  AX.X, ALU.max, negate=True)
                ins.then_inc(cmax_made, 1)

            def cross_norm(h):
                dve.wait_ge(cexp_made, TT * (h + 1))
                nc.vector.reciprocal(crec[:, h, :], csum[:, h, :]).then_inc(crec_made, 1)
                dve.wait_ge(crec_made, h + 1)
                for t in range(TT):
                    nc.vector.tensor_scalar(pr[h % 2][:, t, :], pr[h % 2][:, t, :], crec[:, h, t:t + 1], None,
                                            ALU.mult).then_inc(cp_made, 1)

            def cross_turn1(h):
                dve.wait_ge(ct_done, MT * h + 2)
                if h >= 2:
                    dve.wait_ge(co_done, 2 * (h - 1))
                nc.vector.tensor_copy(prT[h % 2][:, 1, :], pX[1][:, :]).then_inc(ct_read1, 1)

            def cross_out_lo(h):
                for d in range(2):
                    dve.wait_ge(co_hi, 2 * h + d + 1)
                    nc.vector.tensor_tensor(mix_lo[:, 2 * h + d, :], pA[d][:, :], mix_hi[:, 2 * h + d, :].bitcast(F32),
                                            ALU.subtract).then_inc(co_lo, 1)

            for i in range(KT):
                convert(U_MQ + i + AHEAD)
                gains(0, i // 2, i % 2)
                if i == 4:
                    cross_max(0)
                if i == 6:
                    cross_norm(0)
                    cross_max(1)
            cross_norm(1)
            cross_turn1(0)
            for h in range(MHEADS):
                if h + 2 < MHEADS:
                    cross_max(h + 2)
                if h + 1 < MHEADS:
                    cross_turn1(h + 1)
                if h + 2 < MHEADS:
                    cross_norm(h + 2)
                cross_out_lo(h)

            convert(U_MO + AHEAD)
            for t in range(TT - 1):
                residual(TT + t, 0)
            for u in range(3):
                convert(U_MO + RING + u)
            residual(2 * TT - 1, 0)
            convert(U_MO + RING + 3)
            normalize(TT + 0)
            normalize(TT + 1)
            turn2(G_LN2, 0)
            normalize(TT + 2)
            turn2(G_LN2, 1)
            convert(U_UP)
            convert(U_UP + 1)
            normalize(TT + 3)
            turn2(G_LN2, 2)
            convert(U_UP + 2)
            turn2(G_LN2, 3)

            def ffn_tap(y, ps, tap, col, ready, n, signal):
                back = FK - 1 - tap
                dve.wait_ge(ready, n + 1)
                nc.vector.scalar_tensor_tensor(y[:, back:SEQ], ps[:, 0:SEQ - back], fp[:, tap, col:col + 1],
                                               y[:, back:SEQ], ALU.mult, ALU.add).then_inc(signal, 1)

            def ffn_gate(i):
                b = i % 2
                dve.wait_ge(silu_made, i + 1)
                nc.vector.tensor_tensor(yv[b][:, :], yv[b][:, :], yg[b][:, :], ALU.mult).then_inc(gm_made, 1)
                dve.wait_ge(gm_made, i + 1)
                nc.vector.tensor_copy(g_hi[:, i, :], yv[b][:, :]).then_inc(ghi_made, 1)
                dve.wait_ge(ghi_made, i + 1)
                nc.vector.tensor_tensor(g_lo[:, i, :], yv[b][:, :], g_hi[:, i, :].bitcast(F32),
                                        ALU.subtract).then_inc(glo_made, 1)

            for i in range(FT):
                b = i % 2
                convert(U_UP + 2 * i + AHEAD)
                ffn_tap(yv[b], bank[2 * b], 1, i, yv_made, i, tv1)
                convert(U_UP + 2 * i + 1 + AHEAD)
                ffn_tap(yg[b], bank[2 * b + 1], 1, FT + i, yg_made, i, tg1)
                ffn_tap(yv[b], bank[2 * b], 0, i, tv1, i, tv2)
                if i == FT - 1:
                    convert(U_DN + AHEAD)
                ffn_tap(yg[b], bank[2 * b + 1], 0, FT + i, tg1, i, tg2)
                if i:
                    ffn_gate(i - 1)
                if 1 <= i <= 2 * TT:
                    gains(1, (i - 1) // 2, (i - 1) % 2)
            ffn_gate(FT - 1)

            last = DN_HALF % RING
            for u in range(U_DN + RING, U_DN + DN_HALF + RING - last):
                convert(u)
            for t in range(TT - 1):
                residual(2 * TT + t, 0)
            for u in range(U_DN + DN_HALF + RING - last, U_DN + DN_HALF + RING - 1):
                convert(u)
            residual(3 * TT - 1, 0)
            for u in range(U_DN + DN_HALF + RING - 1, NU):
                convert(u)
            for t in range(TT):
                last_norm(2 * TT + t)

        @block.tensor
        def _(pe):
            def turn(g, src):
                if 6 <= g < G_MEM:
                    pe.wait_ge(tr_lo, g - 5)
                if g >= G_LN1 and (g - G_LN1) % (2 * TT) in (4, 5):
                    pe.wait_ge(tr_lo, g - 3)
                for k in range(4):
                    c0 = (4 * (g % 2) + k) * P
                    ins = nc.tensor.transpose(turn_bank(g)[:, k * P:(k + 1) * P], src[:, c0:c0 + P], ident[:, :])
                ins.then_inc(tr_done, 1)

            def turn2(g0, t, n):
                pe.wait_ge(norm_made, n + 1)
                turn(g0 + 2 * t, xres[:, t, :])
                turn(g0 + 2 * t + 1, xres[:, t, :])

            def t_tile(u, dst, hi, lo, t0=0, t1=SEQ):
                if hi is mt_hi:
                    t1 = MEM
                dst, hi, lo = dst[:, t0:t1], hi[:, :, t0:t1], lo[:, :, t0:t1]
                s = u % RING
                pe.wait_ge(lo_made, u + 1)
                for k in range(KT):
                    wh, wl = w_hi[s][:, k * P:(k + 1) * P], w_lo[s][:, k * P:(k + 1) * P]
                    nc.tensor.matmul(dst, wh, hi[:, k, :], start=(k == 0), stop=False)
                    nc.tensor.matmul(dst, wh, lo[:, k, :], start=False, stop=False)
                    ins = nc.tensor.matmul(dst, wl, hi[:, k, :], start=False, stop=(k == KT - 1))
                return ins

            def t_proj(u, j, hi, lo):
                b = TILE_BANK[j]
                if tiles_before(j, b):
                    pe.wait_ge(tile_read[b], tiles_before(j, b))
                t_tile(u, pA[b], hi, lo).then_inc(unit_used, 1)

            def tok_part(u, dst, hi, lo, t, k0, first, last):
                s = u % RING
                pe.wait_ge(lo_made, u + 1)
                for kk in range(2):
                    xh, xl = hi[:, k0 + kk, t * P:(t + 1) * P], lo[:, k0 + kk, t * P:(t + 1) * P]
                    wh, wl = w_hi[s][:, kk * H:(kk + 1) * H], w_lo[s][:, kk * H:(kk + 1) * H]
                    nc.tensor.matmul(dst, xh, wh, start=(first and kk == 0), stop=False)
                    nc.tensor.matmul(dst, xh, wl, start=False, stop=False)
                    ins = nc.tensor.matmul(dst, xl, wh, start=False, stop=(last and kk == 1))
                return ins

            def tok_tile(u0, n, t, dst, hi, lo, k0, first, last, done, parts=None):
                for r in range(n):
                    if parts:
                        pe.wait_ge(*parts[r])
                    ins = tok_part(u0 + r, dst, hi, lo, t, k0 + 2 * r, first and r == 0, last and r == n - 1)
                    if t == TT - 1:
                        ins.then_inc(unit_used, 1)
                if t < TT - 1 and last:
                    ins.then_inc(done, 1)

            def tok_half(u0, half, t, hi, lo, parts=None):
                if half % 2:
                    pe.wait_ge(tok_read, TT * (half - 1) + t + 1)
                tok_tile(u0, RING, t, pT[t][:, :], hi, lo, 0, True, True, tok_done, parts)

            pe.wait_ge(consts_made, 8)
            for t in range(TT):
                pe.wait_ge(x_loaded[t], 16)
                turn(2 * t, xres[:, t, :])
                turn(2 * t + 1, xres[:, t, :])
            cut = SEQ // 2
            pe.wait_ge(tr_lo, TT)
            t_tile(0, pA[0], xt_hi, xt_lo, 0, cut)
            pe.wait_ge(tr_lo, 2 * TT)
            t_tile(0, pA[0], xt_hi, xt_lo, cut, SEQ).then_inc(unit_used, 1)
            for c in range(CT):
                if c:
                    pe.wait_ge(sig_made, c)
                    t_tile(2 * c, pA[0], xt_hi, xt_lo).then_inc(unit_used, 1)
                    pe.wait_ge(u_made, c)
                t_tile(2 * c + 1, pA[1], xt_hi, xt_lo).then_inc(unit_used, 1)
                if c == 0:
                    pe.wait_ge(rows_loaded, 16 * 10)
                    for i in range(CT):
                        nc.tensor.transpose(pT[0][:, i * CONV_K:(i + 1) * CONV_K], cw_rows[:, i * P:(i + 1) * P],
                                            ident[0:CONV_K, 0:CONV_K])
                    nc.tensor.transpose(pT[1][:, 0:3 * CT], cp_rows[:, :], ident[0:3 * CT, 0:3 * CT])
                    nc.tensor.transpose(pT[1][:, P:P + 4 * KT], lp_rows[:, :], ident[0:4 * KT, 0:4 * KT])
                    for k in range(FK + 1):
                        ins = nc.tensor.transpose(pT[2][:, k * 2 * FT:(k + 1) * 2 * FT], fp_rows[:, k, :],
                                                  ident[0:2 * FT, 0:2 * FT])
                    ins.then_inc(rows_turned, 1)
            pe.wait_ge(mem_loaded, 16)
            pe.wait_ge(params_ready, 4)
            for t in range(MT):
                turn(G_MEM + 2 * t, memtok[:, t, :])
                turn(G_MEM + 2 * t + 1, memtok[:, t, :])
            for i in range(2 * TT):
                if i < 2:
                    pe.wait_ge((sig_made, u_made)[i], CT)
                t_proj(U_QK + i, J_QK + i, xt_hi, xt_lo)
            def scores(h):
                p0 = HD * (h % 2)
                for j in (0, 1, 3, 2):
                    b, c0, _ = SEG[j]
                    n = SEQ - j * P
                    nc.tensor.matmul(zbank(h, b)[:, c0:c0 + n], kT[p0:p0 + HD, h // 2, j * P:(j + 1) * P],
                                     qT[p0:p0 + HD, h // 2, j * P:SEQ], start=(j != 3), stop=False,
                                     skip_group_check=True)
                for j in (0, 1, 3, 2):
                    b, c0, _ = SEG[j]
                    ins = nc.tensor.matmul(zbank(h, b)[:, c0:c0 + P], ident_r[:, :], hide_r[:, :], start=False,
                                           stop=True, skip_group_check=True)
                    if j != 1:
                        ins.then_inc(z_done, 1)

            def sums(h):
                pe.wait_ge(splo_made, 3 * (h + 1))
                for j in (0, 1, 3, 2):
                    b, c0, _ = SEG[j]
                    for jj in range(j, TT):
                        s0, n = SEG[jj][2], SEQ - jj * P
                        w = negtri_r if jj == j else negone_r
                        o = zbank(h, b)[:, c0 + (jj - j) * P:c0 + (jj - j) * P + n]
                        nc.tensor.matmul(o, w[:, :], sp_hi[h % 2][:, s0:s0 + n], start=False, stop=False,
                                         skip_group_check=True)
                        ins = nc.tensor.matmul(o, w[:, :], sp_lo[h % 2][:, s0:s0 + n], start=False, stop=True,
                                               skip_group_check=True)
                    if j != 1:
                        ins.then_inc(s_done, 1)

            def head_out(h):
                pe.wait_ge(a_made, 3 * (h + 1))
                if h:
                    pe.wait_ge(pv_lo, h)
                p0 = HD * (h % 2)
                for j in range(TT):
                    s0, n = SEG[j][2], SEQ - j * P
                    ins = nc.tensor.matmul(pA[0][p0:p0 + HD, j * P:SEQ], vtok[:, j, h * HD:(h + 1) * HD],
                                           A[h % 2][:, s0:s0 + n], start=(j == 0), stop=(j == TT - 1),
                                           skip_group_check=True)
                ins.then_inc(pv_done, 1)

            def conv_average(src, done):
                for c in range(CT):
                    ins = nc.tensor.matmul(pA[1][:, :], avg[:, :], src[:, c, :], start=(c == 0), stop=(c == CT - 1))
                ins.then_inc(done, 1)

            pe.wait_ge(tr_lo, G_LN1)
            for t in range(TT):
                tok_tile(U_V, RING, t, pT[t][:, :], xt_hi, xt_lo, 0, True, True, v_done)
            pe.wait_ge(consts_round, 4)
            for i in range(KT - LATE):
                t_proj(U_MK + i, J_MK + i, mt_hi, mt_lo)
                if i == 0:
                    pe.wait_ge(v_read, TT)
                    for b in range(2):
                        pe.wait_ge(tile_read[b], tiles_before(J_MK, b))
                    scores(0)
                if i == 3:
                    scores(1)

            def mem_value(u0, r, banks, tiles=range(MT)):
                for m in tiles:
                    ins = tok_part(u0 + r, banks[m][:, :], mt_hi, mt_lo, m, 2 * r, r == 0, r == RING - 1)
                if MT - 1 in tiles:
                    ins.then_inc(unit_used, 1)

            banks = (pA[1], pX[0])
            for h in range(HEADS):
                sums(h)
                if h < LATE:
                    i = KT - LATE + h
                    t_proj(U_MK + i, J_MK + i, mt_hi, mt_lo)
                if h == 1:
                    pe.wait_ge(tile_read[0], tiles_before(J_MQ, 0))
                if h:
                    head_out(h - 1)
                if h == H_MEAN:
                    pe.wait_ge(tap_done, CT * (CONV_K + 1))
                    pe.wait_ge(tile_read[1], tiles_before(J_MQ, 1))
                    conv_average(cacc, cmean_done)
                if h == H_VAR:
                    pe.wait_ge(csq_made, CT)
                    conv_average(csq, cvar_done)
                if h == 6:
                    pe.wait_ge(cve_made, 1)
                    for r in range(RING):
                        mem_value(U_MV0, r, banks, [0])
                if h + 2 < HEADS:
                    pe.wait_ge(a_made, 3 * (h + 1))
                    scores(h + 2)
            for r in range(RING):
                if r == RING // 2:
                    head_out(HEADS - 1)
                mem_value(U_MV0, r, banks, [1])

            parts = [(clo_made, 2), (clo_made, 4), (pv_lo, 4), (pv_lo, HEADS)]
            for t in range(TT):
                tok_half(U_OUT, 0, t, mix_hi, mix_lo, parts if t == 0 else None)
            def half_and_turns(u0, half, g0, n0):
                for t in range(TT - 1):
                    tok_half(u0, half, t, mix_hi, mix_lo)
                    if t:
                        turn2(g0, t - 1, n0 + t - 1)
                t = TT - 1
                pe.wait_ge(tok_read, TT * (half - 1) + t + 1)
                tok_tile(u0, 2, t, pT[t][:, :], mix_hi, mix_lo, 0, True, False, tok_done)
                turn2(g0, t - 1, n0 + t - 1)
                tok_tile(u0 + 2, 2, t, pT[t][:, :], mix_hi, mix_lo, 4, False, True, tok_done)

            pe.wait_ge(mv_read, MT)
            half_and_turns(U_OUT + RING, 1, G_LN1, 0)
            pe.wait_ge(tr_lo, G_LN1 + 4)
            for r in range(RING):
                mem_value(U_MV1, r, pT)
                if r == 1:
                    turn2(G_LN1, 3, 3)
            def cross_scores(h):
                if h >= 2:
                    pe.wait_ge(cexp_made, TT * (h - 1))
                for t in range(TT):
                    for d in range(2):
                        k = 2 * h + d
                        ins = nc.tensor.matmul(pT[2 * (h % 2) + t // 2][:, MEM * (t % 2):MEM * (t % 2) + MEM],
                                               mqT[:, k, t * P:(t + 1) * P], mkT[:, k, :],
                                               start=(d == 0), stop=(d == 1))
                    if t % 2:
                        ins.then_inc(cs_done, 1)

            def cross_turn(h):
                pe.wait_ge(cp_made, TT * (h + 1))
                if h:
                    pe.wait_ge(ct_read0, h)
                    pe.wait_ge(ct_read1, h)
                for m in range(MT):
                    for t in range(TT):
                        ins = nc.tensor.transpose(pX[m][:, t * P:(t + 1) * P], pr[h % 2][:, t, m * P:(m + 1) * P],
                                                  ident[:, :])
                    ins.then_inc(ct_done, 1)

            def cross_out(h):
                pe.wait_ge(ct_read0, h + 1)
                pe.wait_ge(ct_read1, h + 1)
                for d in range(2):
                    if h:
                        pe.wait_ge(co_lo, 2 * (h - 1) + d + 1)
                    c0 = h * MHD + d * P
                    for m in range(MT):
                        ins = nc.tensor.matmul(pA[d][:, :], mvtok[:, m, c0:c0 + P], prT[h % 2][:, m, :],
                                               start=(m == 0), stop=(m == MT - 1))
                    ins.then_inc(co_done, 1)

            pe.wait_ge(tr_lo, G_LN2)
            for i in range(KT):
                t_proj(U_MQ + i, J_MQ + i, xt_hi, xt_lo)
                if i == 3:
                    pe.wait_ge(mv_read, 2 * MT)
                if i in (3, 5):
                    for b in range(2):
                        pe.wait_ge(tile_read[b], tiles_before(J_MQ + i - 1, b))
                    cross_scores(i // 2 - 1)

            for b in range(2):
                pe.wait_ge(tile_read[b], tiles_before(J_MQ + KT, b))
            cross_turn(0)
            for h in range(MHEADS):
                if h + 2 < MHEADS:
                    cross_scores(h + 2)
                if h + 1 < MHEADS:
                    cross_turn(h + 1)
                cross_out(h)

            for t in range(TT):
                tok_half(U_MO, 2, t, mix_hi, mix_lo, [(co_lo, 2 * (r + 1)) for r in range(RING)] if t == 0 else None)
            half_and_turns(U_MO + RING, 3, G_LN2, TT)

            pe.wait_ge(tr_lo, G_LN2 + TT)
            for u in range(AHEAD):
                t_tile(U_UP + u, bank[u], xt_hi, xt_lo, 0, cut)
                if u == 1:
                    turn2(G_LN2, 3, TT + 3)
            pe.wait_ge(tr_lo, G_LN2 + 2 * TT)
            for u in range(AHEAD):
                t_tile(U_UP + u, bank[u], xt_hi, xt_lo, cut, SEQ).then_inc(unit_used, 1)
            for i in range(1, FT):
                if i >= 2:
                    pe.wait_ge(tv2, i - 1)
                    t_tile(U_UP + 2 * i, bank[2 * (i % 2)], xt_hi, xt_lo).then_inc(unit_used, 1)
                    pe.wait_ge(tg2, i - 1)
                t_tile(U_UP + 2 * i + 1, bank[2 * (i % 2) + 1], xt_hi, xt_lo).then_inc(unit_used, 1)

            for hf in range(2):
                for r0 in range(0, DN_HALF, RING):
                    n = min(RING, DN_HALF - r0)
                    if hf == 0:
                        pe.wait_ge(glo_made, 2 * (r0 + n))
                    for t in range(TT):
                        if hf and r0 == 0:
                            pe.wait_ge(tok_read, 4 * TT + t + 1)
                        tok_tile(U_DN + hf * DN_HALF + r0, n, t, tok_bank(2, t)[:, :], g_hi, g_lo, 2 * r0,
                                 r0 == 0, r0 + n == DN_HALF, tok_done)


_INS = ['x', 'mem', 'w_in', 'conv_w', 'conv_b', 'conv_ln_g', 'conv_ln_b', 'w_out', 'ln1_g', 'ln1_b',
        'mem_wq', 'mem_wk', 'mem_wv', 'mem_wo', 'ln2_g', 'ln2_b',
        'ffn_up', 'ffn_conv_w', 'ffn_conv_b', 'ffn_down', 'ln3_g', 'ln3_b']


def kernel(**inputs):
    import numpy as _np
    import concourse.bacc as _bacc
    from concourse import mybir as _mybir
    from concourse.bass_utils import run_bass_kernel_spmd as _run

    nc = _bacc.Bacc("TRN2", target_bir_lowering=False, num_devices=1)
    arrays, args = {}, []
    for name in _INS:
        a = _np.ascontiguousarray(inputs[name])
        arrays[f"in_{name}_dram"] = a
        args.append(nc.dram_tensor(f"in_{name}_dram", a.shape, _mybir.dt.from_np(a.dtype), kind="ExternalInput").ap())
    shape = inputs["x"].shape
    args.append(nc.dram_tensor("out_dram", shape, _mybir.dt.float32, kind="ExternalOutput").ap())
    decoder_layer(nc, *args)
    r = _run(nc, [arrays], core_ids=[0])
    return r.results[0]["out_dram"]
```

```python
from contextlib import ExitStack

import concourse.bass as bass
from concourse import mybir

F32 = mybir.dt.float32
F32R = mybir.dt.float32r
U8 = mybir.dt.uint8
ALU = mybir.AluOpType
ACT = mybir.ActivationFunctionType
AX = mybir.AxisListType

P = 128
NEG = -1.0e30


def decoder_layer(nc, x, mem, w_in, conv_w, conv_b, conv_ln_g, conv_ln_b, w_out, ln1_g, ln1_b,
                  mem_wq, mem_wk, mem_wv, mem_wo, ln2_g, ln2_b,
                  ffn_up, ffn_conv_w, ffn_conv_b, ffn_down, ln3_g, ln3_b, out):
    _, SEQ, D = x.shape
    MEM = mem.shape[1]
    CONV_K, CH = conv_w.shape[1], conv_w.shape[2]
    FK, FF2 = ffn_conv_w.shape[1], ffn_conv_w.shape[2]
    FF = FF2 // 2
    HEADS, HD = 8, (D - CH) // 8
    MHEADS = 4
    MHD = D // MHEADS
    ALPHA = 2.0 ** 0.25
    EPS = 1e-5
    KT = D // P
    TT = SEQ // P
    MT = MEM // P
    CT = CH // P
    FT = FF // P
    H = D // 2
    QOFF, KOFF, VOFF = 2 * CH, 2 * CH + HEADS * HD, 2 * CH + 2 * HEADS * HD
    PAD = CONV_K - 1
    UP = SEQ + PAD

    RING = 4
    AHEAD = RING - 1
    UW = KT * P

    def t_unit(w, c0):
        return w[0, :, c0:c0 + P].rearrange("(k p) n -> p k n", p=P)

    def tok_unit(w, r, c0):
        return w[0, r * 2 * P:(r + 1) * 2 * P, c0:c0 + H].rearrange("(k p) n -> p k n", p=P)

    units = []
    for c in range(CT):
        units += [t_unit(w_in, CH + c * P), t_unit(w_in, c * P)]
    U_QK = len(units)
    units += [t_unit(w_in, QOFF + i * P) for i in range(2 * HEADS * HD // P)]
    U_V = len(units)
    units += [tok_unit(w_in, r, VOFF) for r in range(KT // 2)]
    U_MK = len(units)
    units += [t_unit(mem_wk, i * P) for i in range(KT)]
    U_MV0 = len(units)
    units += [tok_unit(mem_wv, r, 0) for r in range(KT // 2)]
    U_OUT = len(units)
    units += [tok_unit(w_out, r, hf * H) for hf in range(2) for r in range(KT // 2)]
    U_MV1 = len(units)
    units += [tok_unit(mem_wv, r, H) for r in range(KT // 2)]
    U_MQ = len(units)
    units += [t_unit(mem_wq, i * P) for i in range(KT)]
    U_MO = len(units)
    units += [tok_unit(mem_wo, r, hf * H) for hf in range(2) for r in range(KT // 2)]
    U_UP = len(units)
    units += [None] * (2 * FT)
    U_DN = len(units)
    units += [tok_unit(ffn_down, r, hf * H) for hf in range(2) for r in range(FT // 2)]
    NU = len(units)
    DN_HALF = FT // 2
    Q_UP = U_UP // RING
    assert U_UP % RING == 0 and FT % 2 == 0

    with ExitStack() as ctx:
        def sem(name):
            return ctx.enter_context(nc.semaphore(name))

        SLAB = 207 * 1024
        SB0 = nc.lookup_mloc(ctx.enter_context(nc.sbuf_tensor("slab", [P, SLAB], U8))).addr
        at_ = [0]

        def place(name, shape, dt=F32, at=None):
            n = 4
            for s in shape[1:]:
                n *= s
            if at is None:
                at = at_[0]
                at_[0] += (n + 63) // 64 * 64
            assert at + n <= SLAB, (name, at, n)
            return nc.alloc_sbuf_tensor_at(name, shape, dt, offset=SB0 + at)

        w_raw = [place(f"w_raw{s}", [P, UW]) for s in range(RING)]
        w_hi = [place(f"w_hi{s}", [P, UW], F32R) for s in range(RING)]
        w_lo = [place(f"w_lo{s}", [P, UW], F32R) for s in range(RING)]
        xres = place("xres", [P, TT, D])
        xt_at = at_[0]
        xt_hi = place("xt_hi", [P, KT, SEQ], F32R)
        xt_lo = place("xt_lo", [P, KT, SEQ], F32R)
        ident = place("ident", [P, P])
        avg = place("avg", [P, P])
        ident_r = place("ident_r", [P, P], F32R)
        negtri_r = place("negtri_r", [P, P], F32R)
        negone_r = place("negone_r", [P, P], F32R)
        hide_r = place("hide_r", [P, P], F32R)
        cw = place("cw", [P, CT, CONV_K])
        cp = place("cp", [P, 3 * CT])
        fp = place("fp", [P, FK + 1, 2 * FT])
        lp = place("lp", [P, 4, KT])
        stats = place("stats", [P, TT, 12])
        mv = place("mv", [P, TT, 2])
        vareps = place("vareps", [P, TT])
        lnvar = place("lnvar", [P, TT])
        rstd = place("rstd", [P, TT])
        cmx = place("cmx", [P, MHEADS, TT])
        csum = place("csum", [P, MHEADS, TT])
        crec = place("crec", [P, MHEADS, TT])
        ln_gb = place("ln_gb", [P, 2, D])
        codd = nc.alloc_sbuf_tensor_at("codd", [P, SEQ], F32, offset=SB0 + at_[0] - 4 * 2 * D)
        reg = at_[0]
        KB = 1024
        qT = place("qT", [P, HEADS // 2, SEQ], at=reg)
        kT = place("kT", [P, HEADS // 2, SEQ], at=reg + 8 * KB)
        vtok = place("vtok", [P, TT, HEADS * HD], at=reg + 16 * KB)
        mix_hi = place("mix_hi", [P, KT, SEQ], F32R, at=reg + 24 * KB)
        mix_lo = place("mix_lo", [P, KT, SEQ], F32R, at=reg + 40 * KB)
        mt_hi = place("mt_hi", [P, KT, MEM], F32R, at=reg + 56 * KB)
        mt_lo = place("mt_lo", [P, KT, MEM], F32R, at=reg + 64 * KB)
        mkT = place("mkT", [P, KT, MEM], at=reg + 72 * KB)
        memtok = place("memtok", [P, MT, D], at=reg + 72 * KB)
        cacc = place("cacc", [P, CT, SEQ], at=reg + 80 * KB)
        upad = place("upad", [P, CT, UP], at=reg + 88 * KB)
        csq = place("csq", [P, CT, SEQ], at=reg + 88 * KB)
        cw_rows = place("cw_rows", [CONV_K, CH], at=reg + 24 * KB)
        cp_rows = place("cp_rows", [3 * CT, P], at=reg + 27 * KB)
        fp_rows = place("fp_rows", [2 * FT, FK + 1, P], at=reg + 28 * KB)
        lp_rows = place("lp_rows", [4 * KT, P], at=reg + 31 * KB)
        negtri = place("negtri", [P, P], at=reg + 44 * KB)
        negone = place("negone", [P, P], at=reg + 45 * KB)
        hide = place("hide", [P, P], at=reg + 46 * KB)
        sig = place("sig", [P, SEQ], at=reg + 40 * KB)
        crstd = place("crstd", [P, SEQ], at=reg + 40 * KB)
        SW = 1280
        E = [place(f"E{i}", [P, SW], at=xt_at + 5 * KB * i) for i in range(2)]
        sp_lo = [place(f"sp_lo{i}", [P, SW], F32R, at=xt_at + 5 * KB * i) for i in range(2)]
        sp_hi = [place(f"sp_hi{i}", [P, SW], F32R, at=xt_at + 5 * KB * (2 + i)) for i in range(2)]
        A = [place(f"A{i}", [P, SW], at=xt_at + 5 * KB * (4 + i)) for i in range(2)]
        xaff = [place(f"xaff{i}", [P, 4, P], at=reg + (80 + 2 * i) * KB) for i in range(2)]
        mv_hi = place("mv_hi", [P, MT, D], F32R, at=reg)
        mv_lo = place("mv_lo", [P, MT, D], F32R, at=reg + 88 * KB)
        mk_hi = place("mk_hi", [P, KT, MEM], F32R, at=reg + 80 * KB)
        mk_lo = place("mk_lo", [P, KT, MEM], F32R, at=reg + 72 * KB)
        mq_hi = place("mq_hi", [P, KT, SEQ], F32R, at=reg + 8 * KB)
        mq_lo = place("mq_lo", [P, KT, SEQ], F32R, at=reg + 40 * KB)
        pr = [place(f"pr{i}", [P, TT, MEM], at=reg + (56 + 4 * i) * KB) for i in range(2)]
        prT_hi = [place(f"prT_hi{i}", [P, MT, SEQ], F32R, at=xt_at + 4 * i * KB) for i in range(2)]
        prT_lo = [place(f"prT_lo{i}", [P, MT, SEQ], F32R, at=xt_at + (8 + 4 * i) * KB) for i in range(2)]
        g_hi = place("g_hi", [P, FT, SEQ], F32R, at=reg)
        g_lo = place("g_lo", [P, FT, SEQ], F32R, at=reg + 4 * FT * SEQ)
        f0 = reg + 8 * FT * SEQ
        yv = [place(f"yv{i}", [P, SEQ], at=f0 + 2 * KB * i) for i in range(2)]
        yg = [place(f"yg{i}", [P, SEQ], at=f0 + 2 * KB * (2 + i)) for i in range(2)]

        bank = [ctx.enter_context(nc.psum_tensor(f"bank{i}", [P, SEQ], F32)) for i in range(8)]
        pA = bank[0:2]
        pT = bank[2:6]
        pX = bank[6:8]

        x_loaded = [sem(f"x_loaded{t}") for t in range(TT)]
        raw_loaded = [sem(f"raw_loaded{s}") for s in range(RING)]
        tile_read = [sem("tile_read0"), sem("tile_read1")]
        centred, last_made = sem("centred"), sem("last_made")
        mem_loaded, rows_loaded, ln_loaded, stored = sem("mem_loaded"), sem("rows_loaded"), sem("ln_loaded"), sem("stored")
        w_hi_made, w_lo_made, unit_used = sem("w_hi_made"), sem("w_lo_made"), sem("unit_used")
        consts_made, consts_round, pad_zeroed, rows_turned = sem("consts_made"), sem("consts_round"), sem("pad_zeroed"), sem("rows_turned")
        params_ready = sem("params_ready")
        turned, turned_hi_made, turned_lo_made, affine0_made = sem("turned"), sem("turned_hi_made"), sem("turned_lo_made"), sem("affine0_made")
        affine1_made = sem("affine1_made")
        sig_made, u_made, tap_done, conv_mean_done = sem("sig_made"), sem("u_made"), sem("tap_done"), sem("conv_mean_done")
        conv_centred, conv_squared, conv_var_done, conv_vareps_made = sem("conv_centred"), sem("conv_squared"), sem("conv_var_done"), sem("conv_vareps_made")
        conv_lnvar_made, conv_rstd_made, conv_normed, conv_swished = sem("conv_lnvar_made"), sem("conv_rstd_made"), sem("conv_normed"), sem("conv_swished")
        conv_hi_made, conv_lo_made = sem("conv_hi_made"), sem("conv_lo_made")
        values_done, values_read, z_done, abs_made = sem("values_done"), sem("values_read"), sem("z_done"), sem("abs_made")
        exp_made, log_made, softplus_made, softplus_hi_made = sem("exp_made"), sem("log_made"), sem("softplus_made"), sem("softplus_hi_made")
        softplus_lo_made, sums_done, weights_made, head_done = sem("softplus_lo_made"), sem("sums_done"), sem("weights_made"), sem("head_done")
        head_hi_made, head_lo_made = sem("head_hi_made"), sem("head_lo_made")
        tok_done, tok_read, stats_made, moments_made = sem("tok_done"), sem("tok_read"), sem("stats_made"), sem("moments_made")
        vareps_made, lnvar_made, rstd_made, normed = sem("vareps_made"), sem("lnvar_made"), sem("rstd_made"), sem("normed")
        gain_made, ln_done = sem("gain_made"), sem("ln_done")
        mem_values_hi_made, mem_values_read, mem_keys_hi_made, mem_keys_lo_made = sem("mem_values_hi_made"), sem("mem_values_read"), sem("mem_keys_hi_made"), sem("mem_keys_lo_made")
        mem_queries_lo_made, cross_scores_done, cross_max_made, cross_exp_made = sem("mem_queries_lo_made"), sem("cross_scores_done"), sem("cross_max_made"), sem("cross_exp_made")
        cross_recip_made, cross_prob_made, cross_turned, probs_hi_made = sem("cross_recip_made"), sem("cross_prob_made"), sem("cross_turned"), sem("probs_hi_made")
        probs_lo_made, cross_out_done, cross_hi_made, cross_lo_made = sem("probs_lo_made"), sem("cross_out_done"), sem("cross_hi_made"), sem("cross_lo_made")
        value_tap2_done, gate_tap2_done, value_tap1_done, gate_tap1_done = sem("value_tap2_done"), sem("gate_tap2_done"), sem("value_tap1_done"), sem("gate_tap1_done")
        value_tap0_done, gate_tap0_done, silu_made, gated_made = sem("value_tap0_done"), sem("gate_tap0_done"), sem("silu_made"), sem("gated_made")
        gated_hi_made, gated_lo_made = sem("gated_hi_made"), sem("gated_lo_made")

        LATE = 2
        J_QK, J_MK, J_MQ = 0, 2 * TT, 2 * TT + KT
        TILE_BANK = [0, 1] * TT + [0, 1] * ((KT - LATE) // 2) + [1] * LATE + [0, 1] * (KT // 2)

        H_MEAN, H_SQUARE, H_VAR, H_RSTD, H_SILU, H_PARTS = 2, 3, 4, 5, 6, 7

        def tiles_before(j, b):
            return TILE_BANK[:j].count(b)

        G_MEM, G_LN1, G_LN2 = 2 * TT, 2 * TT + 2 * MT, 4 * TT + 2 * MT

        def turn_bank(g):
            if G_MEM <= g < G_LN1:
                return pT[g - G_MEM]
            if g < G_LN1:
                return (pX + pT)[g % 6]
            return (pX[0], pX[1], pT[0], pT[1], pX[0], pX[1], pT[2], pT[3])[(g - G_LN1) % (2 * TT)]

        SEG = {0: (0, 0, 0), 1: (1, 0, 512), 3: (1, 384, 896), 2: (2, 0, 1024)}
        BANKW = [(0, 512), (512, 512), (1024, 256)]

        def zbank(h, b):
            return (pT[0], pT[1], pX[0])[b] if h % 2 == 0 else (pT[2], pT[3], pX[1])[b]

        HALF_END = [U_OUT + RING, U_OUT + 2 * RING, U_MO + RING, U_MO + 2 * RING, U_DN + DN_HALF, U_DN + 2 * DN_HALF]

        def tok_bank(layer, t):
            return bank[4 + t] if layer == 2 else pT[t]

        block = ctx.enter_context(nc.Block())

        @block.sync
        def _(sp):
            def load_into(s, u, src):
                if not isinstance(u, int) or u >= RING:
                    sp.wait_ge(w_lo_made, u - RING + 1)
                k = src.shape[1]
                sp.dma_start(w_raw[s][:, :].rearrange("p (k n) -> p k n", k=k), src).then_inc(raw_loaded[s], 16)

            def load_unit(u):
                load_into(u % RING, u, units[u])

            def load_ln(g, b):
                for i, v in enumerate((g, b)):
                    sp.dma_start(ln_gb[:, i, :], v[0:1, :].broadcast_to([P, D])).then_inc(ln_loaded, 16)

            for t in range(TT):
                if t == TT - 1:
                    load_unit(0)
                sp.dma_start(xres[:, t, :], x[0, t * P:(t + 1) * P, :]).then_inc(x_loaded[t], 16)
            for u in range(1, U_UP):
                load_unit(u)
                if u == 1:
                    sp.dma_start(cw_rows[:, :], conv_w[0]).then_inc(rows_loaded, 16)
                    for i, v in enumerate((conv_b, conv_ln_g, conv_ln_b)):
                        sp.dma_start(cp_rows[i * CT:(i + 1) * CT, :],
                                     v[0].rearrange("(c p) -> c p", p=P)).then_inc(rows_loaded, 16)
                    sp.dma_start(fp_rows[:, 0:FK, :], ffn_conv_w[0].rearrange("k (c p) -> c k p", p=P)).then_inc(rows_loaded, 16)
                    for i, v in enumerate((ln1_g, ln1_b, ln2_g, ln2_b)):
                        sp.dma_start(lp_rows[i * KT:(i + 1) * KT, :],
                                     v[0].rearrange("(c p) -> c p", p=P)).then_inc(rows_loaded, 16)
                    sp.dma_start(fp_rows[:, FK, :], ffn_conv_b[0].rearrange("(c p) -> c p", p=P)).then_inc(rows_loaded, 16)
                if u == RING - 1:
                    sp.dma_start(memtok[:, :, :], mem[0].rearrange("(t p) d -> p t d", p=P)).then_inc(mem_loaded, 16)
                if u == U_OUT:
                    sp.wait_ge(tap_done, CT * (CONV_K + 1))
                    load_ln(ln1_g, ln1_b)
                if u == U_MO + AHEAD:
                    sp.wait_ge(ln_done, TT)
                    load_ln(ln2_g, ln2_b)
            with sp.Fori(0, FT // 2) as j:
                for s in range(RING):
                    c0 = P * (2 * j + s // 2) + FF * (s % 2)
                    load_into(s, U_UP + RING * j + s,
                              ffn_up[0, :, bass.ds(c0, P)].rearrange("(k p) n -> p k n", p=P))
            for u in range(U_DN, NU):
                load_unit(u)
                if u == U_DN + 2 * RING:
                    sp.wait_ge(ln_done, 2 * TT)
                    load_ln(ln3_g, ln3_b)
            for n in range(2 * TT):
                t, cols = n // 2, slice(n % 2 * H, (n % 2 + 1) * H)
                sp.wait_ge(last_made, n + 1)
                sp.dma_start(out[0, t * P:(t + 1) * P, cols], xres[:, t, cols]).then_inc(stored, 16)
            sp.wait_ge(stored, 16 * 2 * TT)

        @block.gpsimd
        def _(pool):
            nc.gpsimd.memset(ident[:, :], 0.0).then_inc(consts_made, 1)
            nc.gpsimd.memset(negtri[:, :], -1.0).then_inc(consts_made, 1)
            nc.gpsimd.memset(negone[:, :], -1.0).then_inc(consts_made, 1)
            nc.gpsimd.memset(hide[:, :], 0.0).then_inc(consts_made, 1)
            nc.gpsimd.memset(avg[:, :], 1.0 / CH).then_inc(consts_made, 1)
            pool.wait_ge(consts_made, 5)
            nc.gpsimd.affine_select(out=ident[:, :], in_=ident[:, :], compare_op=ALU.not_equal, fill=1.0, base=0,
                                    pattern=[[-1, P]], channel_multiplier=1).then_inc(consts_made, 1)
            nc.gpsimd.affine_select(out=negtri[:, :], in_=negtri[:, :], compare_op=ALU.is_ge, fill=0.0, base=0,
                                    pattern=[[-1, P]], channel_multiplier=1).then_inc(consts_made, 1)
            nc.gpsimd.affine_select(out=hide[:, :], in_=hide[:, :], compare_op=ALU.is_gt, fill=NEG, base=0,
                                    pattern=[[1, P]], channel_multiplier=-1).then_inc(consts_made, 1)
            nc.gpsimd.memset(upad[:, :, 0:PAD], 0.0).then_inc(pad_zeroed, 1)

        @block.scalar
        def _(act):
            def convert_in(q, s):
                act.wait_ge(raw_loaded[s], 16 * (q + 1))
                if not isinstance(q, int) or q:
                    act.wait_ge(unit_used, RING * (q - 1) + s + 1)
                nc.scalar.copy(w_hi[s][:, :], w_raw[s][:, :]).then_inc(w_hi_made, 1)

            def convert(u):
                if u < NU:
                    convert_in(u // RING, u % RING)

            def turn_hi(g, dst, t):
                act.wait_ge(turned, g + 1)
                nc.scalar.copy(dst[:, 4 * (g % 2):4 * (g % 2) + 4, t * P:(t + 1) * P],
                               turn_bank(g)[:, :].rearrange("p (k n) -> p k n", k=4)).then_inc(turned_hi_made, 1)

            def tile(u, j, dst, scale=1.0):
                act.wait_ge(unit_used, u + 1)
                n = dst.shape[1]
                b = TILE_BANK[j]
                nc.scalar.activation(dst, pA[b][:, 0:n], ACT.Copy, scale=scale).then_inc(tile_read[b], 1)

            nc.scalar.preload_act_table_set("sigmoid_and_others")
            for t in range(TT):
                if t == TT - 1:
                    convert(0)
                for hf in range(2):
                    turn_hi(2 * t + hf, xt_hi, t)
            for u in range(1, AHEAD):
                convert(u)
            for c in range(CT):
                convert(2 * c + AHEAD)
                act.wait_ge(unit_used, 2 * c + 1)
                if c:
                    act.wait_ge(u_made, c)
                nc.scalar.activation(sig[:, :], pA[0][:, :], ACT.Sigmoid).then_inc(sig_made, 1)
                if c == 0:
                    act.wait_ge(rows_turned, 1)
                    nc.scalar.copy(cw[:, :, :], pT[0][:, 0:CT * CONV_K].rearrange("p (c k) -> p c k", c=CT)).then_inc(params_ready, 1)
                    nc.scalar.copy(cp[:, :], pT[1][:, 0:3 * CT]).then_inc(params_ready, 1)
                    nc.scalar.copy(lp[:, :, :], pT[1][:, P:P + 4 * KT].rearrange("p (i k) -> p i k", i=4)).then_inc(params_ready, 1)
                    nc.scalar.copy(fp[:, :, :], pT[2][:, 0:(FK + 1) * 2 * FT].rearrange("p (k c) -> p k c", k=FK + 1)).then_inc(params_ready, 1)
                convert(2 * c + 1 + AHEAD)
            for t in range(MT):
                for hf in range(2):
                    turn_hi(G_MEM + 2 * t + hf, mt_hi, t)
            act.wait_ge(consts_made, 8)
            for dst, src in ((ident_r, ident), (negtri_r, negtri), (negone_r, negone), (hide_r, hide)):
                nc.scalar.copy(dst[:, :], src[:, :]).then_inc(consts_round, 1)
            for i in range(8):
                convert(U_QK + i + AHEAD)
                dst = (qT if i < 4 else kT)[:, i % 4, :]
                tile(U_QK + i, J_QK + i, dst, HD ** -0.5 if i < 4 else 1.0)
            convert(U_V + AHEAD)
            for t in range(TT):
                if t == TT - 1:
                    for u in range(3):
                        convert(U_V + RING + u)
                if t < TT - 1:
                    act.wait_ge(values_done, t + 1)
                else:
                    act.wait_ge(unit_used, U_V + RING)
                nc.scalar.copy(vtok[:, t, :], pT[t][:, :]).then_inc(values_read, 1)
            def softplus_parts(h):
                for b, (c0, w) in enumerate(BANKW):
                    act.wait_ge(z_done, 3 * h + b + 1)
                    if h >= 2:
                        act.wait_ge(softplus_lo_made, 3 * (h - 1))
                        act.wait_ge(sums_done, 3 * (h - 1))
                    nc.scalar.activation(E[h % 2][:, c0:c0 + w], zbank(h, b)[:, 0:w], ACT.Abs).then_inc(abs_made, 1)
                for b, (c0, w) in enumerate(BANKW):
                    act.wait_ge(abs_made, 3 * h + b + 1)
                    e = E[h % 2][:, c0:c0 + w]
                    nc.scalar.activation(e, e, ACT.Exp, scale=-1.0).then_inc(exp_made, 1)
                for b, (c0, w) in enumerate(BANKW):
                    act.wait_ge(exp_made, 3 * h + b + 1)
                    e = E[h % 2][:, c0:c0 + w]
                    nc.scalar.activation(e, e, ACT.Ln, bias=1.0).then_inc(log_made, 1)

            def weights_of(h):
                for b, (c0, w) in enumerate(BANKW):
                    act.wait_ge(sums_done, 3 * h + b + 1)
                    nc.scalar.activation(A[h % 2][:, c0:c0 + w], zbank(h, b)[:, 0:w], ACT.Exp).then_inc(weights_made, 1)

            def head_out_hi(h):
                act.wait_ge(head_done, h + 1)
                p0 = HD * (h % 2)
                nc.scalar.copy(mix_hi[p0:p0 + HD, CT + h // 2, :], pA[0][p0:p0 + HD, :]).then_inc(head_hi_made, 1)

            nc.scalar.preload_act_table_set("natural_log_exp_and_others")
            for i in range(KT - LATE):
                convert(U_MK + i + AHEAD)
                tile(U_MK + i, J_MK + i, mkT[:, i, :])
                if i == 2:
                    softplus_parts(0)
                if i == 5:
                    softplus_parts(1)
            for h in range(HEADS):
                weights_of(h)
                if h <= LATE:
                    convert(U_MV0 - LATE + h + AHEAD)
                if h < LATE:
                    i = KT - LATE + h
                    tile(U_MK + i, J_MK + i, mkT[:, i, :])
                if h:
                    head_out_hi(h - 1)
                if h == H_SQUARE:
                    for c in range(CT):
                        act.wait_ge(conv_centred, c + 1)
                        nc.scalar.activation(csq[:, c, :], cacc[:, c, :], ACT.Square).then_inc(conv_squared, 1)
                if h == H_RSTD:
                    act.wait_ge(conv_vareps_made, 1)
                    nc.scalar.activation(crstd[:, :], crstd[:, :], ACT.Ln).then_inc(conv_lnvar_made, 1)
                    act.wait_ge(conv_lnvar_made, 1)
                    nc.scalar.activation(crstd[:, :], crstd[:, :], ACT.Exp, scale=-0.5).then_inc(conv_rstd_made, 1)
                if h + 2 < HEADS:
                    softplus_parts(h + 2)
                if h == H_SILU:
                    for c in range(CT):
                        act.wait_ge(conv_normed, c + 1)
                        nc.scalar.activation(cacc[:, c, :], cacc[:, c, :], ACT.Silu, scale=cp[:, CT + c:CT + c + 1],
                                             bias=cp[:, 2 * CT + c:2 * CT + c + 1]).then_inc(conv_swished, 1)
                    nc.scalar.preload_act_table_set("natural_log_exp_and_others")
            convert(U_MV0 + RING)
            convert(U_MV0 + RING + 1)
            head_out_hi(HEADS - 1)
            convert(U_MV0 + RING + 2)
            convert(U_MV0 + RING + 3)

            def mem_values_hi(hf, banks):
                act.wait_ge(unit_used, (U_MV0, U_MV1)[hf] + RING)
                for m in range(MT):
                    nc.scalar.copy(mv_hi[:, m, hf * H:(hf + 1) * H], banks[m][:, :]).then_inc(mem_values_hi_made, 1)

            mem_values_hi(0, (pA[1], pX[0]))

            def ln_rstd(n):
                t = n % TT
                act.wait_ge(vareps_made, n + 1)
                nc.scalar.activation(lnvar[:, t:t + 1], vareps[:, t:t + 1], ACT.Ln).then_inc(lnvar_made, 1)
                act.wait_ge(lnvar_made, n + 1)
                nc.scalar.activation(rstd[:, t:t + 1], lnvar[:, t:t + 1], ACT.Exp, scale=-0.5).then_inc(rstd_made, 1)

            def turn2(g0, t):
                layer = 0 if g0 == G_LN1 else 1
                n = layer * TT + t
                g = g0 + 2 * t
                act.wait_ge(turned, g + 1)
                if n:
                    act.wait_ge(turned_lo_made, G_LN1 + 2 * n - 1)
                for k in range(4):
                    ins = nc.scalar.activation(xaff[0][:, k, :], turn_bank(g)[:, k * P:(k + 1) * P], ACT.Identity,
                                               scale=lp[:, 2 * layer, k:k + 1], bias=lp[:, 2 * layer + 1, k:k + 1])
                ins.then_inc(affine0_made, 1)
                act.wait_ge(affine0_made, n + 1)
                nc.scalar.copy(xt_hi[:, 0:4, t * P:(t + 1) * P], xaff[0][:, :, :]).then_inc(turned_hi_made, 1)
                act.wait_ge(affine1_made, n + 1)
                nc.scalar.copy(xt_hi[:, 4:8, t * P:(t + 1) * P], xaff[1][:, :, :]).then_inc(turned_hi_made, 1)

            for u in range(4):
                convert(U_OUT + RING + u)
            ln_rstd(0)
            ln_rstd(1)
            turn2(G_LN1, 0)
            ln_rstd(2)
            turn2(G_LN1, 1)
            convert(U_MV1)
            convert(U_MV1 + 1)
            ln_rstd(3)
            convert(U_MV1 + 2)
            turn2(G_LN1, 2)
            convert(U_MV1 + 3)
            convert(U_MQ)
            turn2(G_LN1, 3)
            convert(U_MQ + 1)
            convert(U_MQ + 2)
            mem_values_hi(1, pT)
            def cross_exp(h):
                act.wait_ge(cross_max_made, h + 1)
                if h >= 2:
                    act.wait_ge(cross_turned, MT * (h - 1))
                for t in range(TT):
                    nc.scalar.activation(pr[h % 2][:, t, :], pT[2 * (h % 2) + t // 2][:, MEM * (t % 2):MEM * (t % 2) + MEM],
                                         ACT.Exp, bias=cmx[:, h, t:t + 1],
                                         accum_out=csum[:, h, t:t + 1]).then_inc(cross_exp_made, 1)

            def cross_turn_hi(h):
                if h >= 2:
                    act.wait_ge(cross_out_done, 2 * (h - 1))
                for m in range(MT):
                    act.wait_ge(cross_turned, MT * h + m + 1)
                    nc.scalar.copy(prT_hi[h % 2][:, m, :], pX[m][:, :]).then_inc(probs_hi_made, 1)

            def cross_out_hi(h):
                for d in range(2):
                    act.wait_ge(cross_out_done, 2 * h + d + 1)
                    nc.scalar.copy(mix_hi[:, 2 * h + d, :], pA[d][:, :]).then_inc(cross_hi_made, 1)

            for i in range(KT):
                convert(U_MQ + i + AHEAD)
                tile(U_MQ + i, J_MQ + i, mq_hi[:, i, :], MHD ** -0.5)
                if i == 0:
                    for b in range(2):
                        act.wait_ge(tile_read[b], tiles_before(J_MQ, b))
                    act.wait_ge(turned_lo_made, G_LN2)
                    for m in range(2):
                        nc.scalar.copy(mk_hi[:, 4 * m:4 * m + 4, :], mkT[:, 4 * m:4 * m + 4, :]).then_inc(mem_keys_hi_made, 1)
                if i == 5:
                    cross_exp(0)
                if i == 7:
                    cross_exp(1)

            cross_turn_hi(0)
            cross_exp(2)
            for h in range(MHEADS):
                if h + 1 < MHEADS:
                    cross_turn_hi(h + 1)
                if h + 3 < MHEADS:
                    cross_exp(h + 3)
                cross_out_hi(h)

            convert(U_MO + AHEAD)
            for u in range(4):
                convert(U_MO + RING + u)
            ln_rstd(TT + 0)
            ln_rstd(TT + 1)
            turn2(G_LN2, 0)
            ln_rstd(TT + 2)
            turn2(G_LN2, 1)
            convert(U_UP)
            convert(U_UP + 1)
            ln_rstd(TT + 3)
            convert(U_UP + 2)
            turn2(G_LN2, 2)
            turn2(G_LN2, 3)

            def ffn_silu(i, b):
                act.wait_ge(gate_tap0_done, i + 1)
                nc.scalar.activation(yg[b][:, :], yg[b][:, :], ACT.Silu).then_inc(silu_made, 1)

            def ffn_pair(j, b, first=False, last=False):
                i = 2 * j + b
                q, s = Q_UP + j, 2 * b
                convert_in(q + (s + AHEAD) // RING, (s + AHEAD) % RING)
                if not first:
                    act.wait_ge(gated_lo_made, i - 1)
                act.wait_ge(unit_used, RING * q + s + 1)
                nc.scalar.activation(yv[b][:, :], bank[2 * b][:, :], ACT.Identity,
                                     scale=fp[:, FK - 1, bass.ds(i, 1)], bias=fp[:, FK, bass.ds(i, 1)]).then_inc(value_tap2_done, 1)
                convert_in(q + (s + 1 + AHEAD) // RING, (s + 1 + AHEAD) % RING)
                act.wait_ge(unit_used, RING * q + s + 2)
                nc.scalar.activation(yg[b][:, :], bank[2 * b + 1][:, :], ACT.Identity,
                                     scale=fp[:, FK - 1, bass.ds(FT + i, 1)],
                                     bias=fp[:, FK, bass.ds(FT + i, 1)]).then_inc(gate_tap2_done, 1)
                if last:
                    convert(U_DN + AHEAD)
                if not (first and b == 0):
                    ffn_silu(i - 1, 1 - b)

            for b in range(2):
                ffn_pair(0, b, first=True)
            with act.Fori(1, FT // 2 - 1) as j:
                for b in range(2):
                    ffn_pair(j, b)
            for b in range(2):
                ffn_pair(FT // 2 - 1, b, last=(b == 1))
            ffn_silu(FT - 1, 1)
            nc.scalar.preload_act_table_set("natural_log_exp_and_others")
            for u in range(U_DN + RING, NU):
                convert(u)
            for t in range(TT):
                ln_rstd(2 * TT + t)

        @block.vector
        def _(dve):
            def convert_in(q, s):
                dve.wait_ge(w_hi_made, RING * q + s + 1)
                nc.vector.tensor_tensor(w_lo[s][:, :], w_raw[s][:, :], w_hi[s][:, :].bitcast(F32),
                                        ALU.subtract).then_inc(w_lo_made, 1)

            def convert(u):
                if u < NU:
                    convert_in(u // RING, u % RING)

            def turn_lo(g, hi, lo, t):
                dve.wait_ge(turned_hi_made, g + 1)
                k0 = 4 * (g % 2)
                nc.vector.tensor_tensor(lo[:, k0:k0 + 4, t * P:(t + 1) * P],
                                        turn_bank(g)[:, :].rearrange("p (k n) -> p k n", k=4),
                                        hi[:, k0:k0 + 4, t * P:(t + 1) * P].bitcast(F32), ALU.subtract).then_inc(turned_lo_made, 1)

            taps = [(c, j) for c in range(CT) for j in range(CONV_K + 1)]
            at = [0]

            def conv_taps(n):
                for c, j in taps[at[0]:at[0] + n]:
                    y = (cacc[:, c, :], codd[:, :])[j % 2]
                    if j == 0:
                        dve.wait_ge(u_made, c + 1)
                    if at[0] >= 2:
                        dve.wait_ge(tap_done, at[0] - 1 if j < CONV_K else at[0])
                    if j == CONV_K:
                        ins = nc.vector.tensor_tensor(cacc[:, c, :], cacc[:, c, :], codd[:, :], ALU.add)
                    elif j < 2:
                        ins = nc.vector.tensor_scalar(y, upad[:, c, j:j + SEQ], cw[:, c, j:j + 1],
                                                      (cp[:, c:c + 1], 0.0)[j], ALU.mult, ALU.add)
                    else:
                        ins = nc.vector.scalar_tensor_tensor(y, upad[:, c, j:j + SEQ], cw[:, c, j:j + 1], y,
                                                             ALU.mult, ALU.add)
                    ins.then_inc(tap_done, 1)
                    at[0] += 1

            for t in range(TT):
                if t == TT - 1:
                    convert(0)
                for hf in range(2):
                    turn_lo(2 * t + hf, xt_hi, xt_lo, t)
            for u in range(1, AHEAD):
                convert(u)
            dve.wait_ge(pad_zeroed, 1)
            for c in range(CT):
                convert(2 * c + AHEAD)
                if c:
                    conv_taps(6)
                convert(2 * c + 1 + AHEAD)
                dve.wait_ge(unit_used, 2 * c + 2)
                dve.wait_ge(sig_made, c + 1)
                nc.vector.tensor_tensor(upad[:, c, PAD:UP], pA[1][:, :], sig[:, :], ALU.mult).then_inc(u_made, 1)
                if c == 0:
                    dve.wait_ge(params_ready, 4)
                conv_taps(6)
            for t in range(MT):
                for hf in range(2):
                    turn_lo(G_MEM + 2 * t + hf, mt_hi, mt_lo, t)
            for i in range(8):
                convert(U_QK + i + AHEAD)
                conv_taps(5)
            convert(U_V + AHEAD)
            conv_taps(26)
            for u in range(3):
                convert(U_V + RING + u)

            def softplus(h):
                for b, (c0, w) in enumerate(BANKW):
                    dve.wait_ge(log_made, 3 * h + b + 1)
                    e = E[h % 2][:, c0:c0 + w]
                    nc.vector.scalar_tensor_tensor(e, zbank(h, b)[:, 0:w], 0.0, e, ALU.max, ALU.add).then_inc(softplus_made, 1)
                for b, (c0, w) in enumerate(BANKW):
                    dve.wait_ge(softplus_made, 3 * h + b + 1)
                    nc.vector.tensor_copy(sp_hi[h % 2][:, c0:c0 + w], E[h % 2][:, c0:c0 + w]).then_inc(softplus_hi_made, 1)
                for b, (c0, w) in enumerate(BANKW):
                    dve.wait_ge(softplus_hi_made, 3 * h + b + 1)
                    nc.vector.tensor_tensor(sp_lo[h % 2][:, c0:c0 + w], E[h % 2][:, c0:c0 + w],
                                            sp_hi[h % 2][:, c0:c0 + w].bitcast(F32), ALU.subtract).then_inc(softplus_lo_made, 1)

            def head_out_lo(h):
                dve.wait_ge(head_hi_made, h + 1)
                p0 = HD * (h % 2)
                nc.vector.tensor_tensor(mix_lo[p0:p0 + HD, CT + h // 2, :], pA[0][p0:p0 + HD, :],
                                        mix_hi[p0:p0 + HD, CT + h // 2, :].bitcast(F32), ALU.subtract).then_inc(head_lo_made, 1)

            for i in range(KT - LATE):
                convert(U_MK + i + AHEAD)
                if i == 3:
                    softplus(0)
                conv_taps(4 if i < 3 else 1)
            softplus(1)
            conv_taps(3)
            for h in range(HEADS):
                if h == H_MEAN:
                    conv_taps(len(taps))
                if h:
                    head_out_lo(h - 1)
                if h <= LATE:
                    convert(U_MV0 - LATE + h + AHEAD)
                if h == H_MEAN:
                    dve.wait_ge(conv_mean_done, 1)
                    for c in range(CT):
                        nc.vector.tensor_tensor(cacc[:, c, :], cacc[:, c, :], pA[1][:, :], ALU.subtract).then_inc(conv_centred, 1)
                if h == H_VAR:
                    dve.wait_ge(conv_var_done, 1)
                    nc.vector.tensor_scalar(crstd[:, :], pA[1][:, :], EPS, None, ALU.add).then_inc(conv_vareps_made, 1)
                if h == H_RSTD:
                    dve.wait_ge(conv_rstd_made, 1)
                    for c in range(CT):
                        nc.vector.tensor_tensor(cacc[:, c, :], cacc[:, c, :], crstd[:, :], ALU.mult).then_inc(conv_normed, 1)
                if h == H_PARTS:
                    for c in range(CT):
                        dve.wait_ge(conv_swished, c + 1)
                        nc.vector.tensor_copy(mix_hi[:, c, :], cacc[:, c, :]).then_inc(conv_hi_made, 1)
                    for c in range(CT):
                        dve.wait_ge(conv_hi_made, c + 1)
                        nc.vector.tensor_tensor(mix_lo[:, c, :], cacc[:, c, :], mix_hi[:, c, :].bitcast(F32),
                                                ALU.subtract).then_inc(conv_lo_made, 1)
                if h + 2 < HEADS:
                    softplus(h + 2)
                if h < H_MEAN:
                    conv_taps(3)
            convert(U_MV0 + RING)
            convert(U_MV0 + RING + 1)
            head_out_lo(HEADS - 1)
            convert(U_MV0 + RING + 2)
            convert(U_MV0 + RING + 3)

            def mem_values_lo(hf, banks):
                for m in range(MT):
                    dve.wait_ge(mem_values_hi_made, MT * hf + m + 1)
                    cols = slice(hf * H, (hf + 1) * H)
                    nc.vector.tensor_tensor(mv_lo[:, m, cols], banks[m][:, :], mv_hi[:, m, cols].bitcast(F32),
                                            ALU.subtract).then_inc(mem_values_read, 1)

            mem_values_lo(0, (pA[1], pX[0]))

            def residual(n, hf):
                t = n % TT
                half = 2 * (n // TT) + hf
                idx = half * TT + t
                if t < TT - 1:
                    dve.wait_ge(tok_done, (TT - 1) * half + t + 1)
                else:
                    dve.wait_ge(unit_used, HALF_END[half])
                if half and hf == 0:
                    dve.wait_ge(ln_done, TT * (n // TT - 1) + t + 1)
                xs = xres[:, t, hf * H:(hf + 1) * H]
                nc.vector.scalar_tensor_tensor(xs, xs, ALPHA, tok_bank(n // TT, t)[:, :], ALU.mult, ALU.add).then_inc(tok_read, 1)
                dve.wait_ge(tok_read, idx + 1)
                nc.vector.bn_stats(stats[:, t, 6 * hf:6 * hf + 6], xs).then_inc(stats_made, 1)
                return idx

            def moments(n):
                t = n % TT
                idx = residual(n, 1)
                dve.wait_ge(stats_made, idx + 1)
                nc.vector.bn_aggr(mv[:, t, :], stats[:, t, :]).then_inc(moments_made, 1)
                dve.wait_ge(moments_made, n + 1)
                nc.vector.tensor_scalar(vareps[:, t:t + 1], mv[:, t, 1:2], EPS, None, ALU.add).then_inc(vareps_made, 1)

            def normalize(n):
                moments(n)
                t = n % TT
                dve.wait_ge(rstd_made, n + 1)
                nc.vector.tensor_scalar(xres[:, t, :], xres[:, t, :], mv[:, t, 0:1], rstd[:, t:t + 1],
                                        ALU.subtract, ALU.mult).then_inc(normed, 1)

            def gains(layer, t, i):
                n = layer * TT + t
                if i == 0:
                    dve.wait_ge(turned, (G_LN1, G_LN2)[layer] + 2 * t + 2)
                    dve.wait_ge(ln_loaded, 32 * (layer + 1))
                    nc.vector.tensor_tensor(xres[:, t, :], xres[:, t, :], ln_gb[:, 0, :], ALU.mult).then_inc(gain_made, 1)
                else:
                    dve.wait_ge(gain_made, n + 1)
                    nc.vector.tensor_tensor(xres[:, t, :], xres[:, t, :], ln_gb[:, 1, :], ALU.add).then_inc(ln_done, 1)

            def last_norm(n):
                moments(n)
                t = n % TT
                if t == 0:
                    dve.wait_ge(ln_loaded, 32 * 3)
                halves = [slice(hf * H, (hf + 1) * H) for hf in range(2)]
                for cols in halves:
                    nc.vector.scalar_tensor_tensor(xres[:, t, cols], xres[:, t, cols], mv[:, t, 0:1], ln_gb[:, 0, cols],
                                                   ALU.subtract, ALU.mult).then_inc(centred, 1)
                dve.wait_ge(rstd_made, n + 1)
                for hf, cols in enumerate(halves):
                    dve.wait_ge(centred, 2 * t + hf + 1)
                    nc.vector.scalar_tensor_tensor(xres[:, t, cols], xres[:, t, cols], rstd[:, t:t + 1], ln_gb[:, 1, cols],
                                                   ALU.mult, ALU.add).then_inc(last_made, 1)

            def turn2(g0, t):
                layer = 0 if g0 == G_LN1 else 1
                g = g0 + 2 * t
                dve.wait_ge(turned, g + 2)
                if g > G_LN1:
                    dve.wait_ge(turned_lo_made, g)
                for k in range(4):
                    ins = nc.vector.tensor_scalar(xaff[1][:, k, :], turn_bank(g + 1)[:, k * P:(k + 1) * P],
                                                  lp[:, 2 * layer, 4 + k:5 + k], lp[:, 2 * layer + 1, 4 + k:5 + k],
                                                  ALU.mult, ALU.add)
                ins.then_inc(affine1_made, 1)
                for hf in range(2):
                    dve.wait_ge(turned_hi_made, g + hf + 1)
                    k0 = 4 * hf
                    nc.vector.tensor_tensor(xt_lo[:, k0:k0 + 4, t * P:(t + 1) * P], xaff[hf][:, :, :],
                                            xt_hi[:, k0:k0 + 4, t * P:(t + 1) * P].bitcast(F32),
                                            ALU.subtract).then_inc(turned_lo_made, 1)

            for t in range(TT - 1):
                residual(t, 0)
            for u in range(3):
                convert(U_OUT + RING + u)
            residual(TT - 1, 0)
            convert(U_OUT + RING + 3)
            normalize(0)
            normalize(1)
            turn2(G_LN1, 0)
            normalize(2)
            turn2(G_LN1, 1)
            convert(U_MV1)
            convert(U_MV1 + 1)
            normalize(3)
            convert(U_MV1 + 2)
            turn2(G_LN1, 2)
            convert(U_MV1 + 3)
            convert(U_MQ)
            turn2(G_LN1, 3)
            convert(U_MQ + 1)
            convert(U_MQ + 2)
            mem_values_lo(1, pT)

            def cross_max(h):
                for i in range(2):
                    dve.wait_ge(cross_scores_done, 2 * h + i + 1)
                    ins = nc.vector.tensor_reduce(cmx[:, h, 2 * i:2 * i + 2],
                                                  pT[2 * (h % 2) + i][:, :].rearrange("p (t m) -> p t m", t=2),
                                                  AX.X, ALU.max, negate=True)
                ins.then_inc(cross_max_made, 1)

            def cross_norm(h):
                dve.wait_ge(cross_exp_made, TT * (h + 1))
                nc.vector.reciprocal(crec[:, h, :], csum[:, h, :]).then_inc(cross_recip_made, 1)
                dve.wait_ge(cross_recip_made, h + 1)
                for t in range(TT):
                    nc.vector.tensor_scalar(pr[h % 2][:, t, :], pr[h % 2][:, t, :], crec[:, h, t:t + 1], None,
                                            ALU.mult).then_inc(cross_prob_made, 1)

            def cross_turn_lo(h):
                for m in range(MT):
                    dve.wait_ge(probs_hi_made, MT * h + m + 1)
                    nc.vector.tensor_tensor(prT_lo[h % 2][:, m, :], pX[m][:, :], prT_hi[h % 2][:, m, :].bitcast(F32),
                                            ALU.subtract).then_inc(probs_lo_made, 1)

            def query_lo(i):
                b = TILE_BANK[J_MQ + i]
                dve.wait_ge(tile_read[b], tiles_before(J_MQ + i, b) + 1)
                nc.vector.scalar_tensor_tensor(mq_lo[:, i, :], pA[b][:, :], MHD ** -0.5, mq_hi[:, i, :].bitcast(F32),
                                               ALU.mult, ALU.subtract).then_inc(mem_queries_lo_made, 1)

            def cross_out_lo(h):
                for d in range(2):
                    dve.wait_ge(cross_hi_made, 2 * h + d + 1)
                    nc.vector.tensor_tensor(mix_lo[:, 2 * h + d, :], pA[d][:, :], mix_hi[:, 2 * h + d, :].bitcast(F32),
                                            ALU.subtract).then_inc(cross_lo_made, 1)

            for i in range(KT):
                convert(U_MQ + i + AHEAD)
                query_lo(i)
                if i == 0:
                    for m in range(2):
                        dve.wait_ge(mem_keys_hi_made, m + 1)
                        nc.vector.tensor_tensor(mk_lo[:, 4 * m:4 * m + 4, :], mkT[:, 4 * m:4 * m + 4, :],
                                                mk_hi[:, 4 * m:4 * m + 4, :].bitcast(F32), ALU.subtract).then_inc(mem_keys_lo_made, 1)
                gains(0, i // 2, i % 2)
                if i == 4:
                    cross_max(0)
                if i == 6:
                    cross_norm(0)
                    cross_max(1)
            cross_norm(1)
            cross_max(2)
            cross_turn_lo(0)
            cross_max(3)
            for h in range(MHEADS):
                if h + 1 < MHEADS:
                    cross_turn_lo(h + 1)
                if h + 2 < MHEADS:
                    cross_norm(h + 2)
                cross_out_lo(h)

            convert(U_MO + AHEAD)
            for t in range(TT - 1):
                residual(TT + t, 0)
            for u in range(3):
                convert(U_MO + RING + u)
            residual(2 * TT - 1, 0)
            convert(U_MO + RING + 3)
            normalize(TT + 0)
            normalize(TT + 1)
            turn2(G_LN2, 0)
            normalize(TT + 2)
            turn2(G_LN2, 1)
            convert(U_UP)
            convert(U_UP + 1)
            normalize(TT + 3)
            convert(U_UP + 2)
            turn2(G_LN2, 2)
            turn2(G_LN2, 3)

            def ffn_tap(y, ps, tap, col, ready, n, signal):
                back = FK - 1 - tap
                dve.wait_ge(ready, n + 1)
                nc.vector.scalar_tensor_tensor(y[:, back:SEQ], ps[:, 0:SEQ - back], fp[:, tap, bass.ds(col, 1)],
                                               y[:, back:SEQ], ALU.mult, ALU.add).then_inc(signal, 1)

            def ffn_gate(i, b):
                hi_i, lo_i = (g[:, :, :].rearrange("p k n -> p (k n)")[:, bass.ds(SEQ * i, SEQ)] for g in (g_hi, g_lo))
                dve.wait_ge(silu_made, i + 1)
                nc.vector.tensor_tensor(yv[b][:, :], yv[b][:, :], yg[b][:, :], ALU.mult).then_inc(gated_made, 1)
                dve.wait_ge(gated_made, i + 1)
                nc.vector.tensor_copy(hi_i, yv[b][:, :]).then_inc(gated_hi_made, 1)
                dve.wait_ge(gated_hi_made, i + 1)
                nc.vector.tensor_tensor(lo_i, yv[b][:, :], hi_i.bitcast(F32), ALU.subtract).then_inc(gated_lo_made, 1)

            def ffn_pair(j, b, first=False, last=False):
                i = 2 * j + b
                q, s = Q_UP + j, 2 * b
                convert_in(q + (s + AHEAD) // RING, (s + AHEAD) % RING)
                ffn_tap(yv[b], bank[2 * b], 1, i, value_tap2_done, i, value_tap1_done)
                convert_in(q + (s + 1 + AHEAD) // RING, (s + 1 + AHEAD) % RING)
                ffn_tap(yg[b], bank[2 * b + 1], 1, FT + i, gate_tap2_done, i, gate_tap1_done)
                ffn_tap(yv[b], bank[2 * b], 0, i, value_tap1_done, i, value_tap0_done)
                if last:
                    convert(U_DN + AHEAD)
                ffn_tap(yg[b], bank[2 * b + 1], 0, FT + i, gate_tap1_done, i, gate_tap0_done)
                if not (first and b == 0):
                    ffn_gate(i - 1, 1 - b)

            for b in range(2):
                ffn_pair(0, b, first=True)
            with dve.Fori(1, FT // 2 - 1) as j:
                for b in range(2):
                    ffn_pair(j, b)
            for b in range(2):
                ffn_pair(FT // 2 - 1, b, last=(b == 1))
            ffn_gate(FT - 1, 1)
            for i in range(2 * TT):
                gains(1, i // 2, i % 2)

            last = DN_HALF % RING
            for u in range(U_DN + RING, U_DN + DN_HALF + RING - last):
                convert(u)
            for t in range(TT - 1):
                residual(2 * TT + t, 0)
            for u in range(U_DN + DN_HALF + RING - last, U_DN + DN_HALF + RING - 1):
                convert(u)
            residual(3 * TT - 1, 0)
            for u in range(U_DN + DN_HALF + RING - 1, NU):
                convert(u)
            for t in range(TT):
                last_norm(2 * TT + t)

        @block.tensor
        def _(pe):
            def turn(g, src):
                if 6 <= g < G_MEM:
                    pe.wait_ge(turned_lo_made, g - 5)
                if g >= G_LN1 and (g - G_LN1) % (2 * TT) in (4, 5):
                    pe.wait_ge(turned_lo_made, g - 3)
                for k in range(4):
                    c0 = (4 * (g % 2) + k) * P
                    ins = nc.tensor.transpose(turn_bank(g)[:, k * P:(k + 1) * P], src[:, c0:c0 + P], ident[:, :])
                ins.then_inc(turned, 1)

            def turn2(g0, t, n):
                pe.wait_ge(normed, n + 1)
                turn(g0 + 2 * t, xres[:, t, :])
                turn(g0 + 2 * t + 1, xres[:, t, :])

            def t_tile(u, dst, hi, lo, t0=0, t1=SEQ):
                return t_tile_in(u // RING, u % RING, dst, hi, lo, t0, t1)

            def t_tile_in(q, s, dst, hi, lo, t0=0, t1=SEQ):
                if hi is mt_hi:
                    t1 = MEM
                dst, hi, lo = dst[:, t0:t1], hi[:, :, t0:t1], lo[:, :, t0:t1]
                pe.wait_ge(w_lo_made, RING * q + s + 1)
                for k in range(KT):
                    wh, wl = w_hi[s][:, k * P:(k + 1) * P], w_lo[s][:, k * P:(k + 1) * P]
                    nc.tensor.matmul(dst, wh, hi[:, k, :], start=(k == 0), stop=False)
                    nc.tensor.matmul(dst, wh, lo[:, k, :], start=False, stop=False)
                    ins = nc.tensor.matmul(dst, wl, hi[:, k, :], start=False, stop=(k == KT - 1))
                return ins

            def t_proj(u, j, hi, lo):
                b = TILE_BANK[j]
                if tiles_before(j, b):
                    pe.wait_ge(tile_read[b], tiles_before(j, b))
                t_tile(u, pA[b], hi, lo).then_inc(unit_used, 1)

            def tok_part(u, dst, hi, lo, t, k0, first, last):
                s = u % RING
                pe.wait_ge(w_lo_made, u + 1)
                for kk in range(2):
                    xh, xl = hi[:, k0 + kk, t * P:(t + 1) * P], lo[:, k0 + kk, t * P:(t + 1) * P]
                    wh, wl = w_hi[s][:, kk * H:(kk + 1) * H], w_lo[s][:, kk * H:(kk + 1) * H]
                    nc.tensor.matmul(dst, xh, wh, start=(first and kk == 0), stop=False)
                    nc.tensor.matmul(dst, xh, wl, start=False, stop=False)
                    ins = nc.tensor.matmul(dst, xl, wh, start=False, stop=(last and kk == 1))
                return ins

            def tok_tile(u0, n, t, dst, hi, lo, k0, first, last, done, parts=None):
                for r in range(n):
                    if parts:
                        pe.wait_ge(*parts[r])
                    ins = tok_part(u0 + r, dst, hi, lo, t, k0 + 2 * r, first and r == 0, last and r == n - 1)
                    if t == TT - 1:
                        ins.then_inc(unit_used, 1)
                if t < TT - 1 and last:
                    ins.then_inc(done, 1)

            def tok_half(u0, half, t, hi, lo, parts=None):
                if half % 2:
                    pe.wait_ge(tok_read, TT * (half - 1) + t + 1)
                tok_tile(u0, RING, t, pT[t][:, :], hi, lo, 0, True, True, tok_done, parts)

            pe.wait_ge(consts_made, 8)
            for t in range(TT):
                pe.wait_ge(x_loaded[t], 16)
                turn(2 * t, xres[:, t, :])
                turn(2 * t + 1, xres[:, t, :])
            cut = SEQ // 2
            pe.wait_ge(turned_lo_made, TT)
            t_tile(0, pA[0], xt_hi, xt_lo, 0, cut)
            pe.wait_ge(turned_lo_made, 2 * TT)
            t_tile(0, pA[0], xt_hi, xt_lo, cut, SEQ).then_inc(unit_used, 1)
            for c in range(CT):
                if c:
                    pe.wait_ge(sig_made, c)
                    t_tile(2 * c, pA[0], xt_hi, xt_lo).then_inc(unit_used, 1)
                    pe.wait_ge(u_made, c)
                t_tile(2 * c + 1, pA[1], xt_hi, xt_lo).then_inc(unit_used, 1)
                if c == 0:
                    pe.wait_ge(rows_loaded, 16 * 10)
                    for i in range(CT):
                        nc.tensor.transpose(pT[0][:, i * CONV_K:(i + 1) * CONV_K], cw_rows[:, i * P:(i + 1) * P],
                                            ident[0:CONV_K, 0:CONV_K])
                    nc.tensor.transpose(pT[1][:, 0:3 * CT], cp_rows[:, :], ident[0:3 * CT, 0:3 * CT])
                    nc.tensor.transpose(pT[1][:, P:P + 4 * KT], lp_rows[:, :], ident[0:4 * KT, 0:4 * KT])
                    for k in range(FK + 1):
                        ins = nc.tensor.transpose(pT[2][:, k * 2 * FT:(k + 1) * 2 * FT], fp_rows[:, k, :],
                                                  ident[0:2 * FT, 0:2 * FT])
                    ins.then_inc(rows_turned, 1)
            pe.wait_ge(mem_loaded, 16)
            pe.wait_ge(params_ready, 4)
            for t in range(MT):
                turn(G_MEM + 2 * t, memtok[:, t, :])
                turn(G_MEM + 2 * t + 1, memtok[:, t, :])
            for i in range(2 * TT):
                if i < 2:
                    pe.wait_ge((sig_made, u_made)[i], CT)
                t_proj(U_QK + i, J_QK + i, xt_hi, xt_lo)
            def scores(h):
                p0 = HD * (h % 2)
                for j in (0, 1, 3, 2):
                    b, c0, _ = SEG[j]
                    n = SEQ - j * P
                    nc.tensor.matmul(zbank(h, b)[:, c0:c0 + n], kT[p0:p0 + HD, h // 2, j * P:(j + 1) * P],
                                     qT[p0:p0 + HD, h // 2, j * P:SEQ], start=(j != 3), stop=False,
                                     skip_group_check=True)
                for j in (0, 1, 3, 2):
                    b, c0, _ = SEG[j]
                    ins = nc.tensor.matmul(zbank(h, b)[:, c0:c0 + P], ident_r[:, :], hide_r[:, :], start=False,
                                           stop=True, skip_group_check=True)
                    if j != 1:
                        ins.then_inc(z_done, 1)

            def sums(h):
                pe.wait_ge(softplus_lo_made, 3 * (h + 1))
                for j in (0, 1, 3, 2):
                    b, c0, _ = SEG[j]
                    for jj in range(j, TT):
                        s0, n = SEG[jj][2], SEQ - jj * P
                        w = negtri_r if jj == j else negone_r
                        o = zbank(h, b)[:, c0 + (jj - j) * P:c0 + (jj - j) * P + n]
                        nc.tensor.matmul(o, w[:, :], sp_hi[h % 2][:, s0:s0 + n], start=False, stop=False,
                                         skip_group_check=True)
                        ins = nc.tensor.matmul(o, w[:, :], sp_lo[h % 2][:, s0:s0 + n], start=False, stop=True,
                                               skip_group_check=True)
                    if j != 1:
                        ins.then_inc(sums_done, 1)

            def head_out(h):
                pe.wait_ge(weights_made, 3 * (h + 1))
                if h:
                    pe.wait_ge(head_lo_made, h)
                p0 = HD * (h % 2)
                for j in range(TT):
                    s0, n = SEG[j][2], SEQ - j * P
                    ins = nc.tensor.matmul(pA[0][p0:p0 + HD, j * P:SEQ], vtok[:, j, h * HD:(h + 1) * HD],
                                           A[h % 2][:, s0:s0 + n], start=(j == 0), stop=(j == TT - 1),
                                           skip_group_check=True)
                ins.then_inc(head_done, 1)

            def conv_average(src, done):
                for c in range(CT):
                    ins = nc.tensor.matmul(pA[1][:, :], avg[:, :], src[:, c, :], start=(c == 0), stop=(c == CT - 1))
                ins.then_inc(done, 1)

            pe.wait_ge(turned_lo_made, G_LN1)
            for t in range(TT):
                tok_tile(U_V, RING, t, pT[t][:, :], xt_hi, xt_lo, 0, True, True, values_done)
            pe.wait_ge(consts_round, 4)
            for i in range(KT - LATE):
                t_proj(U_MK + i, J_MK + i, mt_hi, mt_lo)
                if i == 0:
                    pe.wait_ge(values_read, TT)
                    for b in range(2):
                        pe.wait_ge(tile_read[b], tiles_before(J_MK, b))
                    scores(0)
                if i == 3:
                    scores(1)

            def mem_value(u0, r, banks, tiles=range(MT)):
                for m in tiles:
                    ins = tok_part(u0 + r, banks[m][:, :], mt_hi, mt_lo, m, 2 * r, r == 0, r == RING - 1)
                if MT - 1 in tiles:
                    ins.then_inc(unit_used, 1)

            banks = (pA[1], pX[0])
            for h in range(HEADS):
                sums(h)
                if h < LATE:
                    i = KT - LATE + h
                    t_proj(U_MK + i, J_MK + i, mt_hi, mt_lo)
                if h == 1:
                    pe.wait_ge(tile_read[0], tiles_before(J_MQ, 0))
                if h:
                    head_out(h - 1)
                if h == H_MEAN:
                    pe.wait_ge(tap_done, CT * (CONV_K + 1))
                    pe.wait_ge(tile_read[1], tiles_before(J_MQ, 1))
                    conv_average(cacc, conv_mean_done)
                if h == H_VAR:
                    pe.wait_ge(conv_squared, CT)
                    conv_average(csq, conv_var_done)
                if h == 6:
                    pe.wait_ge(conv_vareps_made, 1)
                    for r in range(RING):
                        mem_value(U_MV0, r, banks, [0])
                if h + 2 < HEADS:
                    pe.wait_ge(weights_made, 3 * (h + 1))
                    scores(h + 2)
            for r in range(RING):
                if r == RING // 2:
                    head_out(HEADS - 1)
                mem_value(U_MV0, r, banks, [1])

            parts = [(conv_lo_made, 2), (conv_lo_made, 4), (head_lo_made, 4), (head_lo_made, HEADS)]
            for t in range(TT):
                tok_half(U_OUT, 0, t, mix_hi, mix_lo, parts if t == 0 else None)
            def half_and_turns(u0, half, g0, n0):
                for t in range(TT - 1):
                    tok_half(u0, half, t, mix_hi, mix_lo)
                    if t:
                        turn2(g0, t - 1, n0 + t - 1)
                t = TT - 1
                pe.wait_ge(tok_read, TT * (half - 1) + t + 1)
                tok_tile(u0, 2, t, pT[t][:, :], mix_hi, mix_lo, 0, True, False, tok_done)
                turn2(g0, t - 1, n0 + t - 1)
                tok_tile(u0 + 2, 2, t, pT[t][:, :], mix_hi, mix_lo, 4, False, True, tok_done)

            pe.wait_ge(mem_values_read, MT)
            half_and_turns(U_OUT + RING, 1, G_LN1, 0)
            pe.wait_ge(turned_lo_made, G_LN1 + 4)
            for r in range(RING):
                mem_value(U_MV1, r, pT)
                if r == 1:
                    turn2(G_LN1, 3, 3)
            def cross_scores(h):
                if h >= 2:
                    pe.wait_ge(cross_exp_made, TT * (h - 1))
                for t in range(TT):
                    for d in range(2):
                        k = 2 * h + d
                        o = pT[2 * (h % 2) + t // 2][:, MEM * (t % 2):MEM * (t % 2) + MEM]
                        qh, ql = mq_hi[:, k, t * P:(t + 1) * P], mq_lo[:, k, t * P:(t + 1) * P]
                        nc.tensor.matmul(o, qh, mk_hi[:, k, :], start=(d == 0), stop=False)
                        nc.tensor.matmul(o, qh, mk_lo[:, k, :], start=False, stop=False)
                        ins = nc.tensor.matmul(o, ql, mk_hi[:, k, :], start=False, stop=(d == 1))
                    if t % 2:
                        ins.then_inc(cross_scores_done, 1)

            def cross_turn(h):
                pe.wait_ge(cross_prob_made, TT * (h + 1))
                if h:
                    pe.wait_ge(probs_lo_made, MT * h)
                for m in range(MT):
                    for t in range(TT):
                        ins = nc.tensor.transpose(pX[m][:, t * P:(t + 1) * P], pr[h % 2][:, t, m * P:(m + 1) * P],
                                                  ident[:, :])
                    ins.then_inc(cross_turned, 1)

            def cross_out(h):
                pe.wait_ge(probs_lo_made, MT * (h + 1))
                for d in range(2):
                    if h:
                        pe.wait_ge(cross_lo_made, 2 * (h - 1) + d + 1)
                    c0 = h * MHD + d * P
                    for m in range(MT):
                        vh, vl = mv_hi[:, m, c0:c0 + P], mv_lo[:, m, c0:c0 + P]
                        nc.tensor.matmul(pA[d][:, :], vh, prT_hi[h % 2][:, m, :], start=(m == 0), stop=False)
                        nc.tensor.matmul(pA[d][:, :], vh, prT_lo[h % 2][:, m, :], start=False, stop=False)
                        ins = nc.tensor.matmul(pA[d][:, :], vl, prT_hi[h % 2][:, m, :], start=False, stop=(m == MT - 1))
                    ins.then_inc(cross_out_done, 1)

            pe.wait_ge(turned_lo_made, G_LN2)
            for i in range(KT):
                if i >= 2:
                    pe.wait_ge(mem_queries_lo_made, i - 1)
                t_tile(U_MQ + i, pA[i % 2], xt_hi, xt_lo).then_inc(unit_used, 1)
                if i == 3:
                    pe.wait_ge(mem_values_read, 2 * MT)
                    pe.wait_ge(mem_keys_lo_made, 2)
                if i in (3, 5, 7):
                    pe.wait_ge(mem_queries_lo_made, i - 1)
                    cross_scores(i // 2 - 1)

            pe.wait_ge(mem_queries_lo_made, KT)
            cross_turn(0)
            cross_scores(3)
            for h in range(MHEADS):
                if h + 1 < MHEADS:
                    cross_turn(h + 1)
                cross_out(h)

            for t in range(TT):
                tok_half(U_MO, 2, t, mix_hi, mix_lo, [(cross_lo_made, 2 * (r + 1)) for r in range(RING)] if t == 0 else None)
            half_and_turns(U_MO + RING, 3, G_LN2, TT)

            pe.wait_ge(turned_lo_made, G_LN2 + TT)
            for u in range(AHEAD):
                t_tile(U_UP + u, bank[u], xt_hi, xt_lo, 0, cut)
                if u == 1:
                    turn2(G_LN2, 3, TT + 3)
            pe.wait_ge(turned_lo_made, G_LN2 + 2 * TT)
            for u in range(AHEAD):
                t_tile(U_UP + u, bank[u], xt_hi, xt_lo, cut, SEQ).then_inc(unit_used, 1)
            t_tile(U_UP + AHEAD, bank[AHEAD], xt_hi, xt_lo).then_inc(unit_used, 1)
            with pe.Fori(1, FT // 2) as j:
                for s in range(RING):
                    i = 2 * j + s // 2
                    pe.wait_ge((value_tap0_done, gate_tap0_done)[s % 2], i - 1)
                    t_tile_in(Q_UP + j, s, bank[s], xt_hi, xt_lo).then_inc(unit_used, 1)

            for hf in range(2):
                for r0 in range(0, DN_HALF, RING):
                    n = min(RING, DN_HALF - r0)
                    if hf == 0:
                        pe.wait_ge(gated_lo_made, 2 * (r0 + n))
                    for t in range(TT):
                        if hf and r0 == 0:
                            pe.wait_ge(tok_read, 4 * TT + t + 1)
                        tok_tile(U_DN + hf * DN_HALF + r0, n, t, tok_bank(2, t)[:, :], g_hi, g_lo, 2 * r0,
                                 r0 == 0, r0 + n == DN_HALF, tok_done)


_INS = ['x', 'mem', 'w_in', 'conv_w', 'conv_b', 'conv_ln_g', 'conv_ln_b', 'w_out', 'ln1_g', 'ln1_b',
        'mem_wq', 'mem_wk', 'mem_wv', 'mem_wo', 'ln2_g', 'ln2_b',
        'ffn_up', 'ffn_conv_w', 'ffn_conv_b', 'ffn_down', 'ln3_g', 'ln3_b']


def kernel(**inputs):
    import numpy as _np
    import concourse.bacc as _bacc
    from concourse import mybir as _mybir
    from concourse.bass_utils import run_bass_kernel_spmd as _run

    nc = _bacc.Bacc("TRN2", target_bir_lowering=False, num_devices=1)
    arrays, args = {}, []
    for name in _INS:
        a = _np.ascontiguousarray(inputs[name])
        arrays[f"in_{name}_dram"] = a
        args.append(nc.dram_tensor(f"in_{name}_dram", a.shape, _mybir.dt.from_np(a.dtype), kind="ExternalInput").ap())
    shape = inputs["x"].shape
    args.append(nc.dram_tensor("out_dram", shape, _mybir.dt.float32, kind="ExternalOutput").ap())
    decoder_layer(nc, *args)
    r = _run(nc, [arrays], core_ids=[0])
    return r.results[0]["out_dram"]
```
